# Optimizing a Trainium2 kernel written in Bass

```python
import functools
import jax
import jax.numpy as jnp
from jax import lax
import numpy as np

D_MODEL = 1024
BATCH = 1
SEQ = 512
DEPTH = 4

CTX_LEN = 256
GRID_W = 64
N_MIXERS = 3
EPS = 1e-6

GDN_HEAD_DIM = 128
GDN_QK_HEADS = D_MODEL // GDN_HEAD_DIM
GDN_V_HEADS = 2 * GDN_QK_HEADS
GDN_KEY_DIM = GDN_QK_HEADS * GDN_HEAD_DIM
GDN_VAL_DIM = GDN_V_HEADS * GDN_HEAD_DIM
GDN_CONV_DIM = 2 * GDN_KEY_DIM + GDN_VAL_DIM
GDN_IN_DIM = GDN_CONV_DIM + GDN_VAL_DIM + 4 * GDN_V_HEADS
GDN_CONV_WIDTH = 4
GDN_CHUNK = 64

LRU_WIDTH = D_MODEL
LRU_BLOCKS = 8
LRU_BLOCK = LRU_WIDTH // LRU_BLOCKS
LRU_CONV_WIDTH = 4
LRU_C = 8.0

ATT_HEAD_DIM = 64
ATT_Q_HEADS = D_MODEL // ATT_HEAD_DIM
ATT_KV_HEADS = ATT_Q_HEADS // 4
ATT_GROUP = ATT_Q_HEADS // ATT_KV_HEADS
ATT_Q_DIM = ATT_Q_HEADS * ATT_HEAD_DIM
ATT_KV_DIM = ATT_KV_HEADS * ATT_HEAD_DIM
ATT_IN_DIM = 2 * ATT_Q_DIM + 2 * ATT_KV_DIM
ATT_WINDOW = 128
ATT_BLOCK = 128
ROPE_BASE = 10000.0

N_GDN_LAYERS = (DEPTH + 2) // 3
N_LRU_LAYERS = (DEPTH + 1) // 3
N_ATT_LAYERS = DEPTH // 3

kernel_name = "hybrid_gdn_rglru_swa_prefix_dit"

def rmsnorm(x, g):
    xf = x.astype(jnp.float32)
    y = xf * lax.rsqrt(jnp.mean(xf * xf, axis=-1, keepdims=True) + EPS)
    return (y * g.astype(jnp.float32)).astype(x.dtype)

def l2norm(x):
    xf = x.astype(jnp.float32)
    return (xf * lax.rsqrt(jnp.sum(xf * xf, axis=-1, keepdims=True) + 1e-6)).astype(x.dtype)

def centred_dwconv(x, w):
    k_w, ch = w.shape
    left = k_w // 2
    return lax.conv_general_dilated(
        x, w[:, None, :].astype(x.dtype), window_strides=(1,),
        padding=[(left, k_w - 1 - left)], dimension_numbers=("NWC", "WIO", "NWC"),
        feature_group_count=ch)

def gated_delta_chunked(q, k, v, beta, g, s0):
    bn, nh, length, dk = q.shape
    dv = v.shape[-1]
    cs = GDN_CHUNK
    n = length // cs
    f32 = jnp.float32
    q = q.astype(f32).reshape(bn, nh, n, cs, dk)
    k = k.astype(f32).reshape(bn, nh, n, cs, dk)
    v = v.astype(f32).reshape(bn, nh, n, cs, dv)
    beta = beta.astype(f32).reshape(bn, nh, n, cs)
    gc = jnp.cumsum(g.astype(f32).reshape(bn, nh, n, cs), axis=-1)
    idx = jnp.arange(cs)
    incl = idx[:, None] >= idx[None, :]
    strict = idx[:, None] > idx[None, :]
    decay = jnp.exp(jnp.where(incl, gc[..., :, None] - gc[..., None, :], -jnp.inf))
    kb = k * beta[..., None]
    a_mat = jnp.where(strict, jnp.einsum("bhncd,bhnmd->bhncm", kb, k) * decay, 0.0)
    t_mat = a_mat + jnp.eye(cs, dtype=f32)
    rhs = jnp.concatenate([v * beta[..., None], kb * jnp.exp(gc)[..., None]], axis=-1)
    sol = lax.linalg.triangular_solve(t_mat, rhs, left_side=True, lower=True, unit_diagonal=True)
    u, w = sol[..., :dv], sol[..., dv:]
    qk = jnp.einsum("bhncd,bhnmd->bhncm", q, k) * decay
    q_dec = q * jnp.exp(gc)[..., None]
    k_dec = k * jnp.exp(gc[..., -1:] - gc)[..., None]
    chunk_decay = jnp.exp(gc[..., -1])

    def step(s, inp):
        u_i, w_i, qk_i, q_i, k_i, d_i = inp
        v_new = u_i - jnp.einsum("bhcd,bhde->bhce", w_i, s)
        o_i = jnp.einsum("bhcd,bhde->bhce", q_i, s) + jnp.einsum("bhcm,bhme->bhce", qk_i, v_new)
        s = s * d_i[..., None, None] + jnp.einsum("bhcd,bhce->bhde", k_i, v_new)
        return s, o_i

    xs = tuple(jnp.moveaxis(t, 2, 0) for t in (u, w, qk, q_dec, k_dec, chunk_decay))
    s_final, o = lax.scan(step, s0.astype(f32), xs)
    o = jnp.moveaxis(o, 0, 2).reshape(bn, nh, length, dv)
    return o, s_final

def gdn_mixer(h_ctx, h_lat, with_ctx_out, w_in, conv_w, a_log, dt_bias, g_norm, w_out):
    def streams(h):
        bn, length, _ = h.shape
        p = h @ w_in
        qkv = jax.nn.silu(centred_dwconv(p[..., :GDN_CONV_DIM], conv_w))
        z = p[..., GDN_CONV_DIM:GDN_CONV_DIM + GDN_VAL_DIM]
        ab = p[..., GDN_CONV_DIM + GDN_VAL_DIM:].reshape(bn, length, 2, 2, GDN_V_HEADS)
        rep = GDN_V_HEADS // GDN_QK_HEADS
        q = l2norm(qkv[..., :GDN_KEY_DIM].reshape(bn, length, GDN_QK_HEADS, GDN_HEAD_DIM)) * (GDN_HEAD_DIM ** -0.5)
        k = l2norm(qkv[..., GDN_KEY_DIM:2 * GDN_KEY_DIM].reshape(bn, length, GDN_QK_HEADS, GDN_HEAD_DIM))
        v = qkv[..., 2 * GDN_KEY_DIM:].reshape(bn, length, GDN_V_HEADS, GDN_HEAD_DIM)
        q = jnp.repeat(q, rep, axis=2).transpose(0, 2, 1, 3)
        k = jnp.repeat(k, rep, axis=2).transpose(0, 2, 1, 3)
        v = v.transpose(0, 2, 1, 3)
        a = ab[:, :, 0].astype(jnp.float32).transpose(0, 2, 3, 1)
        b = ab[:, :, 1].astype(jnp.float32).transpose(0, 2, 3, 1)
        beta = jax.nn.sigmoid(b)
        g = -jnp.exp(a_log.astype(jnp.float32))[:, :, None] * jax.nn.softplus(a + dt_bias.astype(jnp.float32)[:, :, None])
        return q, k, v, z, beta, g

    qc, kc, vc, zc, bc, gcx = streams(h_ctx)
    ql, kl, vl, zl, bl, gl = streams(h_lat)
    bn = h_lat.shape[0]
    zero = jnp.zeros((bn, GDN_V_HEADS, GDN_HEAD_DIM, GDN_HEAD_DIM), jnp.float32)
    flip = lambda t: jnp.flip(t, axis=2)
    oc_f, s_f = gated_delta_chunked(qc, kc, vc, bc[:, 0], gcx[:, 0], zero)
    ol_f, _ = gated_delta_chunked(ql, kl, vl, bl[:, 0], gl[:, 0], s_f)
    oc_b, s_b = gated_delta_chunked(flip(qc), flip(kc), flip(vc), flip(bc[:, 1]), flip(gcx[:, 1]), zero)
    ol_b, _ = gated_delta_chunked(flip(ql), flip(kl), flip(vl), flip(bl[:, 1]), flip(gl[:, 1]), s_b)

    def finish(o, z):
        bn_, _, length, _ = o.shape
        o = rmsnorm(o.transpose(0, 2, 1, 3), g_norm).reshape(bn_, length, GDN_VAL_DIM)
        return (o.astype(z.dtype) * jax.nn.silu(z)) @ w_out

    y_lat = finish(ol_f + flip(ol_b), zl)
    y_ctx = finish(oc_f + flip(oc_b), zc) if with_ctx_out else None
    return y_ctx, y_lat

def _lin_combine(left, right):
    a1, b1 = left
    a2, b2 = right
    return a1 * a2, a2 * b1 + b2

def rglru_mixer(h_ctx, h_lat, with_ctx_out, w_in, conv_w, conv_b, w_ra, b_ra, w_ri, b_ri, lam, w_out):
    def streams(h):
        p = h @ w_in
        gate = p[..., :LRU_WIDTH]
        u = centred_dwconv(p[..., LRU_WIDTH:], conv_w) + conv_b
        return gate, u

    def coeffs(u, d):
        bn, length, _ = u.shape
        uf = u.astype(jnp.float32)
        ub = uf.reshape(bn, length, LRU_BLOCKS, LRU_BLOCK)
        r = jax.nn.sigmoid(jnp.einsum("blnc,ncd->blnd", ub, w_ra[d].astype(jnp.float32)).reshape(bn, length, LRU_WIDTH) + b_ra[d])
        i = jax.nn.sigmoid(jnp.einsum("blnc,ncd->blnd", ub, w_ri[d].astype(jnp.float32)).reshape(bn, length, LRU_WIDTH) + b_ri[d])
        log_a = -LRU_C * r * jax.nn.softplus(-lam[d].astype(jnp.float32))
        a = jnp.exp(log_a)
        b = jnp.sqrt(-jnp.expm1(2.0 * log_a)) * (i * uf)
        return a, b

    gate_c, uc = streams(h_ctx)
    gate_l, ul = streams(h_lat)

    def direction(d, rev):
        a, b = coeffs(uc, d)
        _, hc = lax.associative_scan(_lin_combine, (a, b), axis=1, reverse=rev)
        h0 = hc[:, 0] if rev else hc[:, -1]
        a, b = coeffs(ul, d)
        acum, hl = lax.associative_scan(_lin_combine, (a, b), axis=1, reverse=rev)
        return hc, hl + acum * h0[:, None, :]

    hc_f, hl_f = direction(0, False)
    hc_b, hl_b = direction(1, True)
    y_lat = ((hl_f + hl_b).astype(gate_l.dtype) * jax.nn.silu(gate_l)) @ w_out
    y_ctx = (((hc_f + hc_b).astype(gate_c.dtype) * jax.nn.silu(gate_c)) @ w_out) if with_ctx_out else None
    return y_ctx, y_lat

def axial_rope_tables(length):
    rows = length // GRID_W
    row = jnp.repeat(jnp.arange(rows), GRID_W)
    col = jnp.tile(jnp.arange(GRID_W), rows)
    n_freq = ATT_HEAD_DIM // 4
    inv = ROPE_BASE ** (-jnp.arange(n_freq, dtype=jnp.float32) / n_freq)
    ang = jnp.concatenate([row[:, None] * inv, col[:, None] * inv], axis=-1)
    return jnp.cos(ang), jnp.sin(ang)

def apply_rope(x, cos, sin):
    half = x.shape[-1] // 2
    xf = x.astype(jnp.float32)
    x1, x2 = xf[..., :half], xf[..., half:]
    return jnp.concatenate([x1 * cos - x2 * sin, x2 * cos + x1 * sin], axis=-1).astype(x.dtype)

def sink_attention(q, k, v, mask, sink):
    s = jnp.einsum("bqhgd,bkhd->bhgqk", q, k).astype(jnp.float32) * (ATT_HEAD_DIM ** -0.5)
    if mask is not None:
        s = jnp.where(mask, s, -jnp.inf)
    mx = jnp.maximum(jnp.max(s, axis=-1, keepdims=True), sink)
    e = jnp.exp(s - mx)
    p = e / (jnp.sum(e, axis=-1, keepdims=True) + jnp.exp(sink - mx))
    return jnp.einsum("bhgqk,bkhd->bqhgd", p.astype(v.dtype), v)

def window_attn_mixer(h_ctx, h_lat, with_ctx_out, w_in, sinks, w_out):
    def streams(h):
        bn, length, _ = h.shape
        p = h @ w_in
        q = p[..., :ATT_Q_DIM].reshape(bn, length, ATT_KV_HEADS, ATT_GROUP, ATT_HEAD_DIM)
        k = p[..., ATT_Q_DIM:ATT_Q_DIM + ATT_KV_DIM].reshape(bn, length, ATT_KV_HEADS, ATT_HEAD_DIM)
        v = p[..., ATT_Q_DIM + ATT_KV_DIM:ATT_Q_DIM + 2 * ATT_KV_DIM].reshape(bn, length, ATT_KV_HEADS, ATT_HEAD_DIM)
        z = p[..., ATT_Q_DIM + 2 * ATT_KV_DIM:]
        return q, k, v, z

    qc, kc, vc, zc = streams(h_ctx)
    ql, kl, vl, zl = streams(h_lat)
    bn, length, _ = h_lat.shape
    lc = h_ctx.shape[1]
    cos, sin = axial_rope_tables(length)
    ql = apply_rope(ql, cos[:, None, None, :], sin[:, None, None, :])
    kl = apply_rope(kl, cos[:, None, :], sin[:, None, :])
    sink = sinks.astype(jnp.float32).reshape(ATT_KV_HEADS, ATT_GROUP)[None, :, :, None, None]

    nb = length // ATT_BLOCK
    pad = ((0, 0), (ATT_BLOCK, ATT_BLOCK), (0, 0), (0, 0))
    kp = jnp.pad(kl, pad)
    vp = jnp.pad(vl, pad)
    q_blocks = jnp.moveaxis(ql.reshape(bn, nb, ATT_BLOCK, ATT_KV_HEADS, ATT_GROUP, ATT_HEAD_DIM), 1, 0)
    qi_loc = jnp.arange(ATT_BLOCK)
    kj_loc = jnp.arange(3 * ATT_BLOCK) - ATT_BLOCK
    ctx_mask = jnp.ones((ATT_BLOCK, lc), bool)

    def block(args):
        bi, qb = args
        start = bi * ATT_BLOCK
        kb = lax.dynamic_slice_in_dim(kp, start, 3 * ATT_BLOCK, axis=1)
        vb = lax.dynamic_slice_in_dim(vp, start, 3 * ATT_BLOCK, axis=1)
        qi = start + qi_loc
        kj = start + kj_loc
        band = (jnp.abs(qi[:, None] - kj[None, :]) <= ATT_WINDOW) & (kj[None, :] >= 0) & (kj[None, :] < length)
        mask = jnp.concatenate([ctx_mask, band], axis=-1)
        return sink_attention(qb, jnp.concatenate([kc, kb], axis=1), jnp.concatenate([vc, vb], axis=1), mask, sink)

    ol = lax.map(block, (jnp.arange(nb), q_blocks))
    ol = jnp.moveaxis(ol, 0, 1).reshape(bn, length, ATT_Q_DIM)
    y_lat = (ol * jax.nn.silu(zl)) @ w_out
    y_ctx = None
    if with_ctx_out:
        oc = sink_attention(qc, kc, vc, None, sink).reshape(bn, lc, ATT_Q_DIM)
        y_ctx = (oc * jax.nn.silu(zc)) @ w_out
    return y_ctx, y_lat

def setup_inputs(seed: int = 0) -> dict:
    key = jax.random.key(seed)
    ks = iter(jax.random.split(key, 40))
    D = D_MODEL

    def nrm(shape, s):
        return jax.random.normal(next(ks), shape, jnp.float32) * s

    def unif(shape, lo, hi):
        return jax.random.uniform(next(ks), shape, jnp.float32, minval=lo, maxval=hi)

    dt = jnp.exp(unif((N_GDN_LAYERS, 2, GDN_V_HEADS), float(np.log(1e-3)), float(np.log(1e-1))))
    a_pow = unif((N_LRU_LAYERS, 2, LRU_WIDTH), 0.9, 0.999)
    sig_lam = a_pow ** (1.0 / LRU_C)
    return {
        "x": nrm((BATCH, SEQ, D), 1.0),
        "c": nrm((BATCH, D), 1.0),
        "ctx": nrm((BATCH, CTX_LEN, D), 1.0),
        "c_ctx": nrm((D,), 1.0),
        "ada_w": nrm((DEPTH, D, 3 * D), 0.5 * D ** -0.5),
        "ada_b": nrm((DEPTH, 3 * D), 0.02),
        "norm_pre": 1.0 + nrm((DEPTH, D), 0.05),
        "norm_post": 1.0 + nrm((DEPTH, D), 0.05),
        "gdn_w_in": nrm((N_GDN_LAYERS, D, GDN_IN_DIM), D ** -0.5),
        "gdn_conv_w": nrm((N_GDN_LAYERS, GDN_CONV_WIDTH, GDN_CONV_DIM), GDN_CONV_WIDTH ** -0.5),
        "gdn_a_log": jnp.log(unif((N_GDN_LAYERS, 2, GDN_V_HEADS), 1.0, 16.0)),
        "gdn_dt_bias": dt + jnp.log(-jnp.expm1(-dt)),
        "gdn_g_norm": 1.0 + nrm((N_GDN_LAYERS, GDN_HEAD_DIM), 0.05),
        "gdn_w_out": nrm((N_GDN_LAYERS, GDN_VAL_DIM, D), GDN_VAL_DIM ** -0.5),
        "lru_w_in": nrm((N_LRU_LAYERS, D, 2 * LRU_WIDTH), D ** -0.5),
        "lru_conv_w": nrm((N_LRU_LAYERS, LRU_CONV_WIDTH, LRU_WIDTH), LRU_CONV_WIDTH ** -0.5),
        "lru_conv_b": nrm((N_LRU_LAYERS, LRU_WIDTH), 0.02),
        "lru_w_ra": nrm((N_LRU_LAYERS, 2, LRU_BLOCKS, LRU_BLOCK, LRU_BLOCK), LRU_BLOCK ** -0.5),
        "lru_b_ra": nrm((N_LRU_LAYERS, 2, LRU_WIDTH), 0.02),
        "lru_w_ri": nrm((N_LRU_LAYERS, 2, LRU_BLOCKS, LRU_BLOCK, LRU_BLOCK), LRU_BLOCK ** -0.5),
        "lru_b_ri": nrm((N_LRU_LAYERS, 2, LRU_WIDTH), 0.02),
        "lru_lam": jnp.log(sig_lam) - jnp.log1p(-sig_lam),
        "lru_w_out": nrm((N_LRU_LAYERS, LRU_WIDTH, D), LRU_WIDTH ** -0.5),
        "att_w_in": nrm((N_ATT_LAYERS, D, ATT_IN_DIM), D ** -0.5),
        "att_sinks": nrm((N_ATT_LAYERS, ATT_Q_HEADS), 0.5),
        "att_w_out": nrm((N_ATT_LAYERS, ATT_Q_DIM, D), ATT_Q_DIM ** -0.5),
    }

def reference(x, c, ctx, c_ctx, ada_w, ada_b, norm_pre, norm_post,
              gdn_w_in, gdn_conv_w, gdn_a_log, gdn_dt_bias, gdn_g_norm, gdn_w_out,
              lru_w_in, lru_conv_w, lru_conv_b, lru_w_ra, lru_b_ra, lru_w_ri, lru_b_ri, lru_lam, lru_w_out,
              att_w_in, att_sinks, att_w_out):
    x_lat, x_ctx = x, ctx
    for i in range(DEPTH):
        kind, j = i % N_MIXERS, i // N_MIXERS
        with_ctx_out = i < DEPTH - 1
        if kind == 0:
            mixer = functools.partial(gdn_mixer, w_in=gdn_w_in[j], conv_w=gdn_conv_w[j], a_log=gdn_a_log[j],
                                      dt_bias=gdn_dt_bias[j], g_norm=gdn_g_norm[j], w_out=gdn_w_out[j])
        elif kind == 1:
            mixer = functools.partial(rglru_mixer, w_in=lru_w_in[j], conv_w=lru_conv_w[j], conv_b=lru_conv_b[j],
                                      w_ra=lru_w_ra[j], b_ra=lru_b_ra[j], w_ri=lru_w_ri[j], b_ri=lru_b_ri[j],
                                      lam=lru_lam[j], w_out=lru_w_out[j])
        else:
            mixer = functools.partial(window_attn_mixer, w_in=att_w_in[j], sinks=att_sinks[j], w_out=att_w_out[j])
        mod = jax.nn.silu(c) @ ada_w[i] + ada_b[i]
        mod_c = jax.nn.silu(c_ctx) @ ada_w[i] + ada_b[i]
        shift, scale, gate = jnp.split(mod[:, None, :], 3, axis=-1)
        shift_c, scale_c, gate_c = jnp.split(mod_c, 3, axis=-1)
        h_lat = rmsnorm(x_lat, norm_pre[i]) * (1.0 + scale) + shift
        h_ctx = rmsnorm(x_ctx, norm_pre[i]) * (1.0 + scale_c) + shift_c
        y_ctx, y_lat = mixer(h_ctx, h_lat, with_ctx_out)
        x_lat = x_lat + gate * rmsnorm(y_lat, norm_post[i])
        if with_ctx_out:
            x_ctx = x_ctx + gate_c * rmsnorm(y_ctx, norm_post[i])
    return x_lat


_drawn_inputs = setup_inputs


def setup_inputs(seed=0):
    import zlib

    import numpy as np

    out = dict(_drawn_inputs(seed))
    spreads = {}
    factors = {'gdn_g_norm': 8.528, 'lru_b_ra': 64.0, 'lru_b_ri': 31.208, 'att_sinks': 8.0}
    for name, (base, spread) in spreads.items():
        noise = np.random.default_rng([zlib.crc32(name.encode()), seed]).standard_normal(out[name].shape)
        drawn = base * np.exp(spread * noise) if base else spread * noise
        out[name] = jnp.asarray(drawn.astype(out[name].dtype))
    for name, factor in factors.items():
        out[name] = (out[name] * factor).astype(out[name].dtype)
    return out
```

```python
from contextlib import ExitStack

import numpy as np

import concourse.bass as bass
from concourse import mybir

F32 = mybir.dt.float32
U32 = mybir.dt.uint32
BF16 = mybir.dt.bfloat16
ACT = mybir.ActivationFunctionType
ALU = mybir.AluOpType
AX = mybir.AxisListType
ds = bass.ds

D = 1024
P = 128
KD = D // P
SEQ, CTX = 512, 256
T = CTX + SEQ
NT = T // P
CT = CTX // P
DEPTH = 4
EPS = 1e-6
PARTS = ((0, CTX), (CTX, T))

GH = 8
GIN = 6208
LEVELS = 7
LRU_N = 8
AKV, AGRP, AHD, WIN = 4, 4, 64, 128
ROPE_BASE, GRID_W = 10000.0, 64
LNEXP = "natural_log_exp_and_others"
BIG = 1e30
LAYERS_RUN = DEPTH


def shape_constants():
    r = np.arange(P)
    ident = np.eye(P)
    ones = np.ones((P, P))
    upper = (r[:, None] <= r[None, :]) * 1.0
    lower = (r[:, None] >= r[None, :]) * 1.0
    cap_f = np.where(upper > 0, 0.0, -BIG)
    cap_b = np.where(lower > 0, 0.0, -BIG)
    half = AHD // 2
    swap = (r // AHD) * AHD + (r % AHD + half) % AHD
    perm = np.eye(P)[swap]
    t = np.arange(SEQ)
    nf = AHD // 4
    inv = ROPE_BASE ** (-np.arange(nf) / nf)
    ang = np.concatenate([(t // GRID_W)[:, None] * inv, (t % GRID_W)[:, None] * inv], axis=1)
    cos = np.cos(ang).T[r % half]
    sin = np.sin(ang).T[r % half] * np.where(r % AHD < half, -1.0, 1.0)[:, None]
    prev = np.where(r[None, :] >= r[:, None], 0.0, -BIG)
    nxt = np.where(r[None, :] <= r[:, None], 0.0, -BIG)
    band = np.concatenate([prev, np.zeros((P, P)), nxt], axis=1)
    cst = np.concatenate([ident, ones, upper, lower, cap_f, cap_b, perm, cos, sin, band], axis=1)
    mask = np.zeros((P, 2, LEVELS, P // 2), np.uint32)
    for lv in range(LEVELS):
        blk = r >> lv
        for par in range(2):
            cols = blk[blk % 2 == par]
            mask[:, par, lv, :] = blk[:, None] == (cols + (1 if par == 0 else -1))[None, :]
    return cst.astype(np.float32), mask.reshape(P, -1)


CST_W = 7 * P + 2 * SEQ + 3 * P
MASK_W = 2 * LEVELS * P // 2


class Sig:

    def __init__(self, env, name, per=1, step=1, loops=1):
        if name not in env.counted:
            sem = env.ctx.enter_context(env.nc.semaphore(name))
            env.counted[name] = [sem, per * step]
            env.raised.append((sem, per * step))
        entry = env.counted[name]
        self.sem, self.base = entry
        self.per, self.step, self.n = per, step, 0
        entry[1] += loops * per * step

    def at(self, h, k=None):
        k = self.per if k is None else k
        return h * (self.per * self.step) + (self.base + k * self.step)

    def next(self, h):
        self.n = self.n % self.per + 1
        return self.at(h, self.n)


def hold(env, eng):
    eng.sem_inc(env.held, 1)


class Env:
    pass


class Views(dict):

    def __getattr__(self, name):
        return self[name]


def build(nc, a):
    ctx = ExitStack()
    with ctx:
        env = Env()
        env.raised = []
        env.nc, env.ctx, env.a, env.counted = nc, ctx, a, {}
        sb = lambda n, s, d=F32: ctx.enter_context(nc.sbuf_tensor(n, s, d))
        env.cst = sb("cst", [P, CST_W])
        env.mask = sb("mask", [P, MASK_W], U32)
        env.vec = sb("vec", [P, 5, P])
        env.mod = sb("mod", [P, DEPTH, 24, 2])
        env.amul = sb("amul", [P, DEPTH, KD, 2])
        env.gmul = sb("gmul", [P, DEPTH, KD, 2])
        env.stat = sb("stat", [P, 8, 16])
        env.epsc = sb("epsc", [P, 4])
        env.identb = sb("identb", [P, P], BF16)
        env.x = sb("x", [P, NT, D])
        env.hT = sb("hT", [P, KD, T])
        env.W = sb("W", [P, 6, KD, P])
        arena_bytes = (nc.sbuf_bytes_remaining() if callable(nc.sbuf_bytes_remaining) else nc.sbuf_bytes_remaining) - 256
        arena_bytes = arena_bytes // 64 * 64
        env.arena_w = arena_bytes // 4
        env.arena = sb("arena", [P, env.arena_w])
        env.ps = ctx.enter_context(nc.psum_tensor("ps", [P, 8, 512], F32))
        env.ident, env.ones, env.upper, env.lower, env.cap_f, env.cap_b, env.perm = (
            env.cst[:, i * P:(i + 1) * P] for i in range(7))
        env.cos, env.sin = (env.cst[:, 7 * P + i * SEQ:7 * P + (i + 1) * SEQ] for i in range(2))
        env.band = env.cst[:, 7 * P + 2 * SEQ:]
        env.m4 = env.mask[:].rearrange("p (two l c) -> p two l c", two=2, l=LEVELS)
        env.held = ctx.enter_context(nc.semaphore("held"))
        env.bar = ctx.enter_context(nc.semaphore("phase_done"))

        phases = [start_phase(env), ada_phase(env)]
        gdn_i = 0
        for l in range(LAYERS_RUN):
            phases.append(norm_phase(env, l))
            if l % 3 == 0:
                phases.append(gdn_phase(env, l, gdn_i))
                gdn_i += 1
            elif l % 3 == 1:
                phases.append(lru_phase(env, l))
            else:
                phases.append(att_phase(env, l))
            phases.append(out_phase(env, l))
        phases.append(store_phase(env))

        def run(kind, eng):
            if kind == "gpsimd":
                for sem, first in env.raised:
                    eng.sem_inc(sem, first)
            for n, ph in enumerate(phases):
                if kind in ph:
                    ph[kind](eng)
                if n + 1 < len(phases):
                    eng.drain().then_inc(env.bar, 1)
                    eng.wait_ge(env.bar, 5 * (n + 1))

        block = ctx.enter_context(nc.Block())

        @block.sync
        def _(sp):
            run("sync", sp)

        @block.tensor
        def _(pe):
            run("tensor", pe)

        @block.scalar
        def _(act):
            run("scalar", act)

        @block.vector
        def _(dve):
            run("vector", dve)

        @block.gpsimd
        def _(pool):
            run("gpsimd", pool)


def carve(env, specs):
    o, out = 0, {}
    for name, shape, *count in specs:
        n = int(np.prod(shape))
        views = []
        for _ in range(count[0] if count else 1):
            v = env.arena[:, o:o + n] if name[-1] != "b" else env.arena[:, o:o + n // 2].bitcast(BF16)
            if len(shape) == 2:
                v = v.rearrange("p (a b) -> p a b", a=shape[0])
            elif len(shape) == 3:
                v = v.rearrange("p (a b c) -> p a b c", a=shape[0], b=shape[1])
            views.append(v)
            o += ((n if name[-1] != "b" else n // 2) + 7) // 8 * 8
        out[name] = views if count else views[0]
    assert o <= env.arena_w, (o, env.arena_w)
    return Views(out)


def flat(ap):
    return ap.rearrange("p a b -> p (a b)")


C_ROW, CCTX_ROW, PRE_ROW, POST_ROW, CB_ROW, BRA_ROW, BRI_ROW = 0, 8, 16, 48, 80, 88, 104
ADAB_ROW, LAM_ROW, GN_ROW = 0, 96, 112


def start_phase(env):
    a = env.a
    v = carve(env, [("rows", (5, P))])
    loads = [("c", 0, C_ROW, 8), ("c_ctx", 0, CCTX_ROW, 8), ("norm_pre", 0, PRE_ROW, 32),
             ("norm_post", 0, POST_ROW, 32), ("lru_conv_b", 0, CB_ROW, 8), ("lru_b_ra", 0, BRA_ROW, 16),
             ("lru_b_ri", 0, BRI_ROW, 16), ("ada_b", 1, ADAB_ROW, 96), ("lru_lam", 1, LAM_ROW, 16),
             ("gdn_g_norm", 1, GN_ROW, 2), ("gdn_conv_w", 2, 0, 256), ("lru_conv_w", 4, 0, 32)]
    n_loads = len(loads) + 4
    loaded = Sig(env, "start_loaded", n_loads + 1, 16)
    cleared = Sig(env, "start_cleared", 1)
    turned = Sig(env, "vec_turned", 1)
    dve_s = Sig(env, "start_dve", 4)
    act_s = Sig(env, "start_act", 2)

    def sync(sp):
        sp.dma_start(env.cst[:], a["cst"]).then_inc(loaded.sem, 16)
        sp.dma_start(env.mask[:], a["mask"]).then_inc(loaded.sem, 16)
        sp.dma_start(env.x[:, 0:CT, :], a["ctx"].rearrange("o (t p) d -> p (o t) d", p=P)).then_inc(loaded.sem, 16)
        sp.dma_start(env.x[:, CT:NT, :], a["x"].rearrange("o (t p) d -> p (o t) d", p=P)).then_inc(loaded.sem, 16)
        sp.wait_ge(cleared.sem, cleared.at(0))
        for name, blk, row, n in loads:
            src = flat_dram(a[name]).rearrange("(r q) -> r q", q=P)
            for i in range(0, n, P):
                m = min(P, n - i)
                sp.dma_start(v.rows[row:row + m, blk + i // P, :], src[i:i + m, :]).then_inc(loaded.sem, 16)

    def vector(dve):
        dve.memset(v.rows, 0.0).then_inc(cleared.sem, 1)
        dve.wait_ge(turned.sem, turned.at(0))
        dve.tensor_copy(env.vec[:, 0:4, :], env.ps[:, 0, :].rearrange("p (a b) -> p a b", a=4)).then_inc(dve_s.sem, 1)
        dve.wait_ge(dve_s.sem, dve_s.next(0))
        dve.tensor_copy(env.vec[:, 4, :], env.ps[:, 1, 0:P]).then_inc(dve_s.sem, 1)
        dve.wait_ge(dve_s.sem, dve_s.next(0))
        dve.tensor_copy(env.identb[:], env.ident).then_inc(dve_s.sem, 1)
        dve.wait_ge(dve_s.sem, dve_s.next(0))
        dve.memset(env.epsc[:, 0:1], EPS).then_inc(dve_s.sem, 1)
        dve.wait_ge(dve_s.sem, dve_s.next(0))
        dve.memset(env.epsc[:, 1:2], EPS * P)
        dve.memset(env.epsc[:, 2:3], 0.0)
        dve.memset(env.epsc[:, 3:4], 1.0)

    def tensor(pe):
        pe.wait_ge(loaded.sem, loaded.at(0))
        for b in range(5):
            mm = pe.transpose(env.ps[:, b // 4, (b % 4) * P:(b % 4 + 1) * P], v.rows[:, b, :], env.ident)
        mm.then_inc(turned.sem, 1)

    def scalar(act):
        act.wait_ge(dve_s.sem, dve_s.at(0))
        c = env.vec[:, 0, 0:16]
        act.activation(c, c, ACT.Silu).then_inc(act_s.sem, 1)
        act.wait_ge(act_s.sem, act_s.next(0))
        act.copy(env.stat[:, 0, 0:16], c).then_inc(act_s.sem, 1)

    return dict(sync=sync, vector=vector, tensor=tensor, scalar=scalar)


def flat_dram(ap):
    n = len(ap.shape)
    names = "abcdefgh"[:n]
    if n == 1:
        return ap
    return ap.rearrange(" ".join(names) + " -> (" + " ".join(names) + ")")


def ada_phase(env):
    NCH = 3 * D // 512
    v = carve(env, [("w", (NCH, KD, 512)), ("cc", (KD, 2))])
    wsem = [Sig(env, f"ada_w{i}", 1, 16, DEPTH) for i in range(NCH)]
    cc_s = Sig(env, "ada_cc", 1)
    used = Sig(env, "ada_used", NCH, 1, DEPTH)
    evac = Sig(env, "ada_evac", NCH, 1, DEPTH)
    fin = Sig(env, "ada_fin", 2 * DEPTH)

    def sync(sp):
        src = env.a["ada_w"].rearrange("l (k p) n -> l p k n", p=P)
        with sp.Fori(0, DEPTH) as h:
            for c in range(NCH):
                sp.wait_ge(used.sem, used.at(h, c + 1 - NCH))
                hold(env, sp)
                sp.dma_start(v.w[:, c], src[ds(h, 1), :, :, c * 512:(c + 1) * 512].rearrange("o p k n -> (o p) k n")
                             ).then_inc(wsem[c].sem, 16)

    def tensor(pe):
        pe.wait_ge(cc_s.sem, cc_s.at(0))
        with pe.Fori(0, DEPTH) as h:
            for c in range(NCH):
                i = c % 2
                pe.wait_ge(wsem[c].sem, wsem[c].at(h))
                pe.wait_ge(evac.sem, evac.at(h, c + 1 - 2))
                for m in range(4):
                    for k in range(KD):
                        mm = pe.matmul(env.ps[:, i, 2 * m:2 * m + 2], v.w[:, c, k, m * P:(m + 1) * P], v.cc[:, k, :],
                                       start=(k == 0), stop=(k == KD - 1))
                mm.then_inc(used.sem, 1)

    def vector(dve):
        dve.tensor_copy(v.cc.rearrange("p k s -> p s k"),
                        env.vec[:, 0, 0:16].rearrange("p (s k) -> p s k", s=2)).then_inc(cc_s.sem, 1)
        dve.wait_ge(cc_s.sem, cc_s.next(0))
        bias = env.vec[:, 1, ADAB_ROW:ADAB_ROW + 96].rearrange("p (l n) -> p l n", l=DEPTH)
        with dve.Fori(0, DEPTH) as h:
            for c in range(NCH):
                dve.wait_ge(used.sem, used.at(h, c + 1))
                for s in range(2):
                    ins = dve.tensor_tensor(env.mod[:, ds(h, 1), 4 * c:4 * c + 4, s],
                                            env.ps[:, c % 2, 0:8].rearrange("p (o m s) -> p s o m", o=1, s=2)[:, s],
                                            bias[:, ds(h, 1), 4 * c:4 * c + 4], ALU.add)
                ins.then_inc(evac.sem, 1)
                dve.wait_ge(evac.sem, evac.next(h))
        for l in range(DEPTH):
            pre = env.vec[:, 0, PRE_ROW + 8 * l:PRE_ROW + 8 * l + 8].unsqueeze(2).broadcast_to([P, KD, 2])
            post = env.vec[:, 0, POST_ROW + 8 * l:POST_ROW + 8 * l + 8].unsqueeze(2).broadcast_to([P, KD, 2])
            dve.scalar_tensor_tensor(env.amul[:, l], env.mod[:, l, 8:16, :], 1.0, pre, ALU.add, ALU.mult).then_inc(fin.sem, 1)
            dve.wait_ge(fin.sem, fin.next(0))
            dve.tensor_tensor(env.gmul[:, l], env.mod[:, l, 16:24, :], post, ALU.mult).then_inc(fin.sem, 1)
            dve.wait_ge(fin.sem, fin.next(0))

    return dict(sync=sync, tensor=tensor, vector=vector)


def norm_phase(env, l):
    v = carve(env, [("xn", (NT, D)), ("junk", (2, D))])
    sq = Sig(env, f"n{l}_sq", NT + 2)
    dv = Sig(env, f"n{l}_dv", 2 + NT)
    tr = Sig(env, f"n{l}_tr", 2 * KD)
    ev_c = Sig(env, f"n{l}_evc", KD)
    ev_l = Sig(env, f"n{l}_evl", KD)
    ssq, var, std, rstd = (env.stat[:, i, 0:NT] for i in range(4))

    def scalar(act):
        for t in range(NT):
            act.activation(v.junk[:, t % 2], env.x[:, t], ACT.Square, accum_out=env.stat[:, 0, t:t + 1]).then_inc(sq.sem, 1)
            act.wait_ge(sq.sem, sq.next(0))
        act.wait_ge(dv.sem, dv.at(0, 1))
        act.activation(std, var, ACT.Sqrt).then_inc(sq.sem, 1)
        act.wait_ge(sq.sem, sq.next(0))
        for k in range(KD):
            act.wait_ge(tr.sem, tr.at(0, 2 * k + 2))
            act.activation(env.hT[:, k, CTX:T], env.ps[:, 2 * (k % 2) + 1, :], ACT.Identity,
                           bias=env.mod[:, l, k, 0:1], scale=env.amul[:, l, k, 0:1]).then_inc(ev_l.sem, 1)
            act.wait_ge(ev_l.sem, ev_l.next(0))

    def vector(dve):
        dve.wait_ge(sq.sem, sq.at(0, NT))
        dve.tensor_scalar(var, ssq, 1.0 / D, EPS, ALU.mult, ALU.add).then_inc(dv.sem, 1)
        dve.wait_ge(dv.sem, dv.next(0))
        dve.wait_ge(sq.sem, sq.at(0, NT + 1))
        dve.reciprocal(rstd, std).then_inc(dv.sem, 1)
        dve.wait_ge(dv.sem, dv.next(0))
        for t in range(NT):
            dve.tensor_scalar(v.xn[:, t], env.x[:, t], env.stat[:, 3, t:t + 1], None, ALU.mult).then_inc(dv.sem, 1)
            dve.wait_ge(dv.sem, dv.next(0))
        for k in range(KD):
            dve.wait_ge(tr.sem, tr.at(0, 2 * k + 1))
            dve.tensor_scalar(env.hT[:, k, 0:CTX], env.ps[:, 2 * (k % 2), 0:CTX], env.amul[:, l, k, 1:2],
                              env.mod[:, l, k, 1:2], ALU.mult, ALU.add).then_inc(ev_c.sem, 1)
            dve.wait_ge(ev_c.sem, ev_c.next(0))

    def tensor(pe):
        pe.wait_ge(dv.sem, dv.at(0))
        for k in range(KD):
            for s, (t0, t1) in enumerate(((0, CT), (CT, NT))):
                if k >= 2:
                    pe.wait_ge((ev_c, ev_l)[s].sem, (ev_c, ev_l)[s].at(0, k - 1))
                for t in range(t0, t1):
                    mm = pe.transpose(env.ps[:, 2 * (k % 2) + s, (t - t0) * P:(t - t0 + 1) * P],
                                      v.xn[:, t, k * P:(k + 1) * P], env.ident)
                mm.then_inc(tr.sem, 1)

    return dict(scalar=scalar, vector=vector, tensor=tensor)


def project(pe, env, slot, banks):
    for b, (t0, t1) in zip(banks, PARTS):
        for k in range(KD):
            mm = pe.matmul(env.ps[:, b, 0:t1 - t0], env.W[:, slot, k, :], env.hT[:, k, t0:t1],
                           start=(k == 0), stop=(k == KD - 1))
    return mm


def ones_sum(pe, env, src, banks):
    for b, (t0, t1) in zip(banks, PARTS):
        mm = pe.matmul(env.ps[:, b, 0:t1 - t0], env.ones, src[:, t0:t1], start=True, stop=True)
    return mm


PADW = T + 6
PAD_AT = (2, 4 + CTX)
CONVW = T + 2


def conv(dve, acc, pad, w, sig, h):
    dve.tensor_scalar(acc[:, 0:CONVW], pad[:, 0:CONVW], w(0), None, ALU.mult).then_inc(sig.sem, 1)
    dve.wait_ge(sig.sem, sig.next(h))
    for j in range(1, 4):
        dve.scalar_tensor_tensor(acc[:, 0:CONVW], pad[:, j:j + CONVW], w(j), acc[:, 0:CONVW],
                                 ALU.mult, ALU.add).then_inc(sig.sem, 1)
        dve.wait_ge(sig.sem, sig.next(h))


def gdn_phase(env, l, j):
    last = l == DEPTH - 1
    a = env.a
    w_in = a["gdn_w_in"][j]
    KINDS = 7
    G, NGC, NB, B, NEG, KDEC, DCH = range(KINDS)
    SPEC = [("pad", (2, PADW)), ("acc", (2, CONVW)), ("q", (T,)), ("k", (T,)), ("vs", (2, T)), ("sq", (T,)),
            ("vtok", (2, NT, P)), ("ktok", (NT, P)), ("sz", (2, T)), ("KK", (NT, P)), ("QK", (NT, P)),
            ("OT", (T,)), ("gt", (T,)), ("cw", (4, 4)), ("sch", (KINDS * NT, 4)),
            ("offdiag", (P,)), ("S", (2, P)), ("R", (2, P)), ("V", (2, P))]
    SPEC += [(n, (NT, P), 2) for n in ("DEC", "NAT", "MF", "MT", "QKD", "QD", "KDX", "Xb", "NATb", "Mb", "MTb")]
    SPEC += [("table", (KINDS * NT, 32))]
    v = carve(env, SPEC)
    arow = flat(v.MF[1])[:, 0:32]
    dtrow = flat(v.MF[1])[:, 32:64]
    nega = flat(v.MF[1])[:, 64:96]
    wab = flat(v.NAT[0])[:, 0:KD * 64].rearrange("p (k n) -> p k n", k=KD)
    DEC, NAT, MF, MT, QKD, QD, KDX = v.DEC, v.NAT, v.MF, v.MT, v.QKD, v.QD, v.KDX
    Xb, NATb, Mb, MTb = v.Xb, v.NATb, v.Mb, v.MTb
    S = lambda n, per=1, step=1: Sig(env, "gdn_" + n, per, step, 1 if n.startswith("tab") else GH)
    t_ld = S("tab_ld", 3, 16)
    t_mm = S("tab_mm", 2)
    t_dve = S("tab_dve", 16)
    t_act = S("tab_act", 8)
    w_ld = [S(f"w_ld{i}", (2, 1, 1, 2)[i], 16) for i in range(4)]
    stage = S("stage", 4)
    proj = S("proj", 6)
    zev = S("zev", 4)
    padw = S("padw", 8)
    convd = S("convd", 16)
    silu = S("silu", 8)
    sqd = S("sqd", 2)
    sums = S("sums", 2)
    rsd = S("rsd", 6)
    strict = S("strict")
    nrm = S("nrm", 2)
    turn = S("turn", 4)
    tev = S("tev", 8)
    ugd = S("ugd", 4)
    kdec = S("kdec", 4 * NT)
    gcm = S("gcm", 4)
    egd = S("egd", 4)
    decd = S("decd", 4)
    dmat = S("dmat", 4 * NT)
    natd = S("natd", 4 * NT)
    minit = S("minit", 8)
    natb = S("natb", 4)
    nati = S("nati", 4)
    qdd = S("qdd", 4)
    qkd = S("qkd", 4)
    m0f = S("m0f", 4)
    rf = S("rf", 16)
    rev = S("rev", 8)
    m1 = S("m1", 8)
    mtb = S("mtb", 4)
    mtf = S("mtf", 4)
    inx = S("inx", 4 * LEVELS)
    inxe = S("inxe", 4 * (LEVELS - 1))
    iny = S("iny", 4 * (LEVELS - 1))
    inm = S("inm", 4 * 2 * LEVELS)
    rks = S("rks", 20)
    rr = S("rr", 20)
    rv = S("rv", 24)
    rve = S("rve", 24)
    ro = S("ro", 24)
    roe = S("roe", 24)
    ru = S("ru", 20)
    rue = S("rue", 20)
    osq = S("osq", 2)
    osum = S("osum", 2)
    ors = S("ors", 6)
    og = S("og", 4)
    st = S("st", 2, 16)
    ZC, KC_, QC, VC = 4096, 1024, 0, 2048
    BW = [1, 0] + list(range(NT - 1, CT - 1, -1))

    def chunk(d, step):
        return step if d == 0 else BW[step]

    first_seen = {}
    for s_ in range(NT):
        for d in range(2):
            first_seen.setdefault(chunk(d, s_), (s_, d))

    def sync(sp):
        sp.dma_start(wab, w_in.rearrange("(k p) n -> p k n", p=P)[:, :, GIN - 64:GIN]).then_inc(t_ld.sem, 16)
        row = lambda t: flat_dram(a[t][j]).partition_broadcast(P)
        sp.dma_start(arow, row("gdn_a_log")).then_inc(t_ld.sem, 16)
        sp.dma_start(dtrow, row("gdn_dt_bias")).then_inc(t_ld.sem, 16)
        wv = w_in.rearrange("(k p) n -> p k n", p=P)

        def load(i, h):
            if i in (0, 3):
                for u in range(2):
                    c = (ZC if i == 0 else VC) + u * P
                    sp.dma_start(env.W[:, (0 if i == 0 else 4) + u], wv[:, :, ds(h * 256 + c, P)]).then_inc(w_ld[i].sem, 16)
            else:
                sp.dma_start(env.W[:, 1 + i], wv[:, :, ds(h * P + (KC_ if i == 1 else QC), P)]).then_inc(w_ld[i].sem, 16)

        def store(h, u):
            sp.wait_ge(og.sem, og.at(h, 2 * u + 2))
            sp.dma_start(a["scratch"][ds(2 * h + u, 1)].rearrange("o p t -> (o p) t"), v.gt).then_inc(st.sem, 16)

        for i in range(4):
            load(i, 0)
        with sp.Fori(0, GH - 1) as h:
            for i, n in enumerate((2, 3, 4, 6)):
                sp.wait_ge(proj.sem, proj.at(h, n))
                hold(env, sp)
                load(i, h + 1)
            for u in range(2):
                store(h, u)
        for u in range(2):
            store(GH - 1, u)
        sp.wait_ge(st.sem, st.at(GH - 1))

    def tensor(pe):
        ps = env.ps
        pe.wait_ge(t_ld.sem, t_ld.at(0))
        for t in range(NT):
            for k in range(KD):
                mm = pe.matmul(ps[:, 0, t * 64:t * 64 + 64], env.hT[:, k, t * P:(t + 1) * P], wab[:, k, :],
                               start=(k == 0), stop=(k == KD - 1))
        mm.then_inc(t_mm.sem, 1)
        tabv = v.table.rearrange("p (k c) n -> p k c n", k=KINDS)
        pe.wait_ge(t_dve.sem, t_dve.at(0, 6))
        pe.matmul(ps[:, 1, 0:96], env.upper, tabv[:, G, :, 0:16], start=True, stop=True)
        pe.matmul(ps[:, 2, 0:96], env.lower, tabv[:, G, :, 16:32], start=True, stop=True)
        pe.matmul(ps[:, 3, 0:192], env.ones, tabv[:, G], start=True, stop=True).then_inc(t_mm.sem, 1)
        pe.wait_ge(t_dve.sem, t_dve.at(0))
        pe.wait_ge(t_act.sem, t_act.at(0))

        with pe.Fori(0, GH) as h:
            bank = 0
            evs = [(zev, 2), (zev, 4), (padw, 2), (padw, 4), (padw, 6), (padw, 8)]
            for n in range(6):
                if n in (0, 2, 3, 4):
                    pe.wait_ge(w_ld[{0: 0, 2: 1, 3: 2, 4: 3}[n]].sem, w_ld[{0: 0, 2: 1, 3: 2, 4: 3}[n]].at(h))
                if n < 2:
                    pe.wait_ge(roe.sem, roe.at(h, 0))
                    pe.wait_ge(rue.sem, rue.at(h, 0))
                    pe.wait_ge(rr.sem, rr.at(h, 0))
                    pe.wait_ge(rve.sem, rve.at(h, 0))
                    pe.wait_ge(ors.sem, ors.at(h, 0))
                else:
                    pe.wait_ge(evs[n - 2][0].sem, evs[n - 2][0].at(h, evs[n - 2][1]))
                project(pe, env, n, (2 * (n % 2), 2 * (n % 2) + 1)).then_inc(proj.sem, 1)
                if n == 4:
                    for i in range(2):
                        pe.wait_ge(sqd.sem, sqd.at(h, i + 1))
                        ones_sum(pe, env, (v.sq, v.gt)[i], (4 + 2 * i, 5 + 2 * i)).then_inc(sums.sem, 1)

            pe.wait_ge(nrm.sem, nrm.at(h, 2))
            pe.wait_ge(rsd.sem, rsd.at(h, 6))
            for c in range(NT):
                mm = pe.transpose(ps[:, 4 + c // 3, (c % 3) * P:(c % 3 + 1) * P], v.k[:, c * P:(c + 1) * P], env.ident)
            mm.then_inc(turn.sem, 1)
            for c in range(NT):
                kc = v.k[:, c * P:(c + 1) * P]
                mm = pe.matmul(ps[:, 6 + c // 3, (c % 3) * P:(c % 3 + 1) * P], kc, kc, start=True, stop=True)
            mm.then_inc(turn.sem, 1)
            pe.wait_ge(padw.sem, padw.at(h, 8))
            for c in range(NT):
                mm = pe.matmul(ps[:, c // 3, (c % 3) * P:(c % 3 + 1) * P], v.k[:, c * P:(c + 1) * P],
                               v.q[:, c * P:(c + 1) * P], start=True, stop=True)
            mm.then_inc(turn.sem, 1)
            for u in range(2):
                pe.wait_ge(silu.sem, silu.at(h, 6 + 2 * u))
                pe.wait_ge(tev.sem, tev.at(h, 2 + 2 * u))
                for c in range(NT):
                    mm = pe.transpose(ps[:, 4 + 2 * u + c // 3, (c % 3) * P:(c % 3 + 1) * P],
                                      v.vs[:, u, c * P:(c + 1) * P], env.ident)
            mm.then_inc(turn.sem, 1)

            for u in range(2):
                for d in range(2):
                    pe.wait_ge(ugd.sem, ugd.at(h, 2 * u + d + 1))
                    if u == 0:
                        pe.wait_ge(tev.sem, tev.at(h, 6))
                    for i in range(2):
                        mm = pe.matmul(ps[:, 2 * d + i, 0:384], env.ones, flat(MF[d])[:, i * 384:(i + 1) * 384],
                                       start=True, stop=True)
                    mm.then_inc(gcm.sem, 1)
                if u == 0:
                    pe.wait_ge(tev.sem, tev.at(h))
                for lv in range(LEVELS):
                    s = 1 << lv
                    for d in range(2):
                        g = 2 * u + d
                        if lv == 0:
                            pe.wait_ge(natd.sem, natd.at(h, (g + 1) * NT))
                            pe.wait_ge(natb.sem, natb.at(h, g + 1))
                        else:
                            pe.wait_ge(inm.sem, inm.at(h, g_inm(u, d, lv - 1)))
                        mcol = half_cols(Mb[d], s, d)
                        icol = env.identb[:].rearrange("p (b two s) -> p b two s", two=2, s=s)[:, :, d, :]
                        for c in range(NT):
                            rhs = icol if lv == 0 else mcol[:, c]
                            mm = pe.matmul(ps[:, 4 * d, c * 64:(c + 1) * 64].rearrange("p (b s) -> p b s", s=s),
                                           NATb[d][:, c], rhs, start=True, stop=True)
                        mm.then_inc(inx.sem, 1)
                    if lv == 0:
                        continue
                    for d in range(2):
                        pe.wait_ge(inxe.sem, inxe.at(h, 2 * (u * (LEVELS - 1) + lv - 1) + d + 1))
                        xcol = half_cols(Xb[d], s, d)
                        tcol = half_cols(MTb[d], s, 1 - d)
                        for c in range(NT):
                            pe.matmul(ps[:, 4 * d + 1, c * 64:(c + 1) * 64].rearrange("p (b s) -> p b s", s=s),
                                      MTb[d][:, c], xcol[:, c], start=True, stop=True)
                            mm = pe.matmul(ps[:, 4 * d + 2, c * 64:(c + 1) * 64].rearrange("p (b s) -> p b s", s=s),
                                           Xb[d][:, c], tcol[:, c], start=True, stop=True)
                        mm.then_inc(iny.sem, 1)

                def residual(d, b0):
                    for c in range(NT):
                        o = unit(b0, c)
                        pe.matmul(o, NAT[d][:, c], MF[d][:, c], start=True, stop=False)
                        mm = pe.matmul(o, env.identb[:], env.identb[:], start=False, stop=True)
                    return mm

                for d in range(2):
                    pe.wait_ge(inm.sem, inm.at(h, g_inm(u, d, LEVELS - 1)))
                    pe.wait_ge(m0f.sem, m0f.at(h, 2 * u + d + 1))
                    pe.wait_ge(nati.sem, nati.at(h, 2 * u + d + 1))
                    residual(d, 4 * d).then_inc(rf.sem, 1)
                for d in range(2):
                    pe.wait_ge(rev.sem, rev.at(h, 4 * u + d + 1))
                    for c in range(NT):
                        pe.matmul(unit(4 * d + 2, c), MTb[d][:, c], Xb[d][:, c], start=True, stop=True)
                        mm = pe.matmul(unit(4 * d, c), Xb[d][:, c], MTb[d][:, c], start=True, stop=True)
                    mm.then_inc(rf.sem, 1)
                for d in range(2):
                    pe.wait_ge(m1.sem, m1.at(h, 4 * u + 2 * d + 2))
                    residual(d, 4 * d + 2).then_inc(rf.sem, 1)
                for d in range(2):
                    pe.wait_ge(rev.sem, rev.at(h, 4 * u + 2 + d + 1))
                    pe.wait_ge(mtb.sem, mtb.at(h, 2 * u + d + 1))
                    for c in range(NT):
                        mm = pe.matmul(unit(4 * d, c), Xb[d][:, c], MTb[d][:, c], start=True, stop=True)
                    mm.then_inc(rf.sem, 1)
                pe.wait_ge(mtf.sem, mtf.at(h, 2 * u + 2))
                pe.wait_ge(qkd.sem, qkd.at(h, 2 * u + 2))
                pe.wait_ge(qdd.sem, qdd.at(h, 2 * u + 2))
                for s_ in range(NT):
                    r = 5 * 2 * u + 2 * (s_ - 1)
                    rb = 2 * NT * u + 2 * s_
                    if s_ > 0:
                        for d in range(2):
                            c = chunk(d, s_)
                            pe.wait_ge(rue.sem, rue.at(h, r + d + 1))
                            pe.matmul(ps[:, 4 * d, 0:P], v.k[:, c * P:(c + 1) * P], v.S[:, d], start=True, stop=True).then_inc(rks.sem, 1)
                    for d in range(2):
                        c = chunk(d, s_)
                        if s_ > 0:
                            pe.wait_ge(rr.sem, rr.at(h, r + d + 1))
                        lhsT = MT[d][:, c]
                        pe.matmul(ps[:, 4 * d + 1, 0:P], lhsT, v.R[:, d] if s_ else v.vtok[:, u, c],
                                  start=True, stop=True).then_inc(rv.sem, 1)
                    for d in range(2):
                        c = chunk(d, s_)
                        pe.wait_ge(rve.sem, rve.at(h, rb + d + 1))
                        if s_ < NT - 1:
                            pe.wait_ge(kdec.sem, kdec.at(h, (2 * u + d + 1) * NT))
                            if s_ == 0:
                                pe.wait_ge(rue.sem, rue.at(h, 10 * u))
                            pe.matmul(ps[:, 4 * d + 2, 0:P], KDX[d][:, c], v.V[:, d], start=True, stop=True).then_inc(ru.sem, 1)
                        pe.wait_ge(roe.sem, roe.at(h, rb + d + 1 - 2))
                        if s_ > 0:
                            pe.matmul(ps[:, 4 * d + 3, 0:P], v.S[:, d], QD[d][:, c], start=True, stop=False)
                        pe.matmul(ps[:, 4 * d + 3, 0:P], v.V[:, d], QKD[d][:, c], start=(s_ == 0), stop=True).then_inc(ro.sem, 1)
                pe.wait_ge(osq.sem, osq.at(h, u + 1))
                pe.wait_ge(rve.sem, rve.at(h, 12 * (u + 1)))
                pe.wait_ge(rr.sem, rr.at(h, 10 * (u + 1)))
                pe.wait_ge(rue.sem, rue.at(h, 10 * (u + 1)))
                ones_sum(pe, env, v.sq, (0, 1)).then_inc(osum.sem, 1)
                pe.wait_ge(ors.sem, ors.at(h, 3 * u + 3))
                pe.wait_ge(roe.sem, roe.at(h, 12 * (u + 1)))

    def unit(b0, c):
        return env.ps[:, b0 + c // 3, (c % 3) * P:(c % 3 + 1) * P]

    def g_inm(u, d, lv):
        return 4 * (u * LEVELS + lv) + 2 * d + 2

    def half_cols(t, s, par):
        return t.rearrange("p c (b two s) -> p c b two s", two=2, s=s)[:, :, :, par, :]

    def scalar(act):
        ps = env.ps
        tabv = v.table.rearrange("p (k c) n -> p k c n", k=KINDS)
        tok = lambda x, w: x.rearrange("p (c n) -> p c n", n=w)
        hold(env, act)
        act.preload_act_table_set(LNEXP)
        act.wait_ge(t_ld.sem, t_ld.at(0))
        act.activation(nega, arow, ACT.Exp).then_inc(t_act.sem, 1)
        act.wait_ge(t_act.sem, t_act.next(0))
        act.wait_ge(t_dve.sem, t_dve.at(0, 2))
        big = flat(v.MF[0])
        A1, E1, L1 = big[:, 192:384], big[:, 384:576], big[:, 576:768]
        act.activation(E1, A1, ACT.Exp, scale=-1.0).then_inc(t_act.sem, 1)
        act.wait_ge(t_act.sem, t_act.next(0))
        act.activation(L1, E1, ACT.Ln, bias=env.epsc[:, 3:4]).then_inc(t_act.sem, 1)
        act.wait_ge(t_act.sem, t_act.next(0))
        act.activation(tabv[:, B], tok(ps[:, 0, 0:384], 64)[:, :, 32:64], ACT.Exp, scale=-1.0).then_inc(t_act.sem, 1)
        act.wait_ge(t_act.sem, t_act.next(0))
        act.wait_ge(t_mm.sem, t_mm.at(0, 2))
        act.wait_ge(t_dve.sem, t_dve.at(0, 12))
        act.activation(tabv[:, NEG], tabv[:, NGC], ACT.Exp, scale=-1.0).then_inc(t_act.sem, 1)
        act.wait_ge(t_act.sem, t_act.next(0))
        act.activation(tabv[:, KDEC], tabv[:, KDEC], ACT.Exp).then_inc(t_act.sem, 1)
        act.wait_ge(t_act.sem, t_act.next(0))
        act.activation(tabv[:, DCH], tok(ps[:, 3, 0:192], 32), ACT.Exp).then_inc(t_act.sem, 1)
        act.wait_ge(t_act.sem, t_act.next(0))
        act.activation(tabv[:, NEG], tabv[:, NEG], ACT.Copy, scale=-1.0).then_inc(t_act.sem, 1)
        act.wait_ge(t_act.sem, t_act.next(0))

        with act.Fori(0, GH) as h:
            for u in range(2):
                act.wait_ge(proj.sem, proj.at(h, u + 1))
                act.wait_ge(og.sem, og.at(h, 0))
                for i, (t0, t1) in enumerate(PARTS):
                    act.activation(v.sz[:, u, t0:t1], ps[:, 2 * u + i, 0:t1 - t0], ACT.Silu).then_inc(zev.sem, 1)
                    act.wait_ge(zev.sem, zev.next(h))

            def pad_and_silu(n, dst, tail):
                if tail is not None:
                    act.wait_ge(convd.sem, convd.at(h, 4 * tail + 4))
                    act.wait_ge(turn.sem, turn.at(h, 0))
                    act.wait_ge(ro.sem, ro.at(h, 0))
                    act.wait_ge(sqd.sem, sqd.at(h, 0))
                    act.wait_ge(nrm.sem, nrm.at(h, 0))
                    act.wait_ge(qdd.sem, qdd.at(h, 0))
                    for t0, t1 in PARTS:
                        o = 0 if t0 == 0 else 2
                        act.activation(dst[:, t0:t1], v.acc[:, tail % 2, t0 + o:t1 + o], ACT.Silu).then_inc(silu.sem, 1)
                        act.wait_ge(silu.sem, silu.next(h))
                if n >= 0:
                    act.wait_ge(proj.sem, proj.at(h, n + 3))
                    act.wait_ge(convd.sem, convd.at(h, 4 * (n - 1)))
                    for i, (t0, t1) in enumerate(PARTS):
                        act.copy(v.pad[:, n % 2, PAD_AT[i]:PAD_AT[i] + t1 - t0],
                                 ps[:, 2 * (n % 2) + i, 0:t1 - t0]).then_inc(padw.sem, 1)
                        act.wait_ge(padw.sem, padw.next(h))

            pad_and_silu(0, None, None)
            pad_and_silu(1, v.k, 0)
            pad_and_silu(2, v.q, 1)
            hold(env, act)
            act.preload_act_table_set(LNEXP)
            for i in range(2):
                act.wait_ge(sums.sem, sums.at(h, i + 1))
                sc = 1.0 if i == 0 else float(P)
                buf = v.sq if i == 0 else v.gt
                for b, (t0, t1) in enumerate(PARTS):
                    act.activation(buf[:, t0:t1], ps[:, 4 + 2 * i + b, 0:t1 - t0], ACT.Ln,
                                   scale=sc, bias=env.epsc[:, i:i + 1]).then_inc(rsd.sem, 1)
                    act.wait_ge(rsd.sem, rsd.next(h))
                act.activation(buf, buf, ACT.Exp, scale=-0.5).then_inc(rsd.sem, 1)
                act.wait_ge(rsd.sem, rsd.next(h))
            pad_and_silu(3, v.vs[:, 0], 2)
            pad_and_silu(-1, v.vs[:, 1], 3)
            hold(env, act)
            act.preload_act_table_set(LNEXP)
            act.wait_ge(kdec.sem, kdec.at(h, 0))
            act.wait_ge(natd.sem, natd.at(h, 0))
            act.wait_ge(qkd.sem, qkd.at(h, 0))
            act.wait_ge(rr.sem, rr.at(h, 0))
            for n, (dst, b0) in enumerate(((v.ktok, 4), (v.KK, 6), (v.QK, 0))):
                act.wait_ge(turn.sem, turn.at(h, n + 1))
                for i in range(2):
                    act.copy(dst[:, 3 * i:3 * i + 3], ps[:, b0 + i, 0:384].rearrange("p (c n) -> p c n", n=P)).then_inc(tev.sem, 1)
                    act.wait_ge(tev.sem, tev.next(h))
            act.wait_ge(turn.sem, turn.at(h, 4))
            for u in range(2):
                act.copy(v.vtok[:, u].rearrange("p (i c) n -> p i c n", i=2),
                         ps[:, 4 + 2 * u:6 + 2 * u, 0:384].rearrange("p i (c n) -> p i c n", n=P)).then_inc(tev.sem, 1)
                act.wait_ge(tev.sem, tev.next(h))
            for u in range(2):
                act.wait_ge(rf.sem, rf.at(h, 8 * u))
                for d in range(2):
                    for t in (Mb[d], MTb[d]):
                        act.copy(t, env.ident.unsqueeze(1).broadcast_to([P, NT, P])).then_inc(minit.sem, 1)
                        act.wait_ge(minit.sem, minit.next(h))
                for d in range(2):
                    act.wait_ge(gcm.sem, gcm.at(h, 2 * u + d + 1))
                    act.activation(QD[d].rearrange("p (i c) n -> p i (c n)", i=2),
                                   ps[:, 2 * d:2 * d + 2, 0:384], ACT.Exp).then_inc(egd.sem, 1)
                    act.wait_ge(egd.sem, egd.next(h))
                for d in range(2):
                    act.wait_ge(dmat.sem, dmat.at(h, (2 * u + d + 1) * NT))
                    act.activation(DEC[d], DEC[d], ACT.Exp).then_inc(decd.sem, 1)
                    act.wait_ge(decd.sem, decd.next(h))
                for d in range(2):
                    act.wait_ge(natd.sem, natd.at(h, (2 * u + d + 1) * NT))
                    act.copy(NATb[d], NAT[d]).then_inc(natb.sem, 1)
                    act.wait_ge(natb.sem, natb.next(h))
                for lv in range(1, LEVELS):
                    for d in range(2):
                        act.wait_ge(inx.sem, inx.at(h, 2 * (u * LEVELS + lv) + d + 1))
                        s = 1 << lv
                        act.copy(half_cols(Xb[d], s, d),
                                 ps[:, 4 * d, 0:384].rearrange("p (c b s) -> p c b s", c=NT, s=s)).then_inc(inxe.sem, 1)
                        act.wait_ge(inxe.sem, inxe.next(h))
                two_banks = lambda b0: ps[:, b0:b0 + 2, 0:384]
                halves = lambda t: t.rearrange("p (i c) n -> p i (c n)", i=2)
                for d in range(2):
                    act.wait_ge(inm.sem, inm.at(h, g_inm(u, d, LEVELS - 1)))
                    act.copy(MF[d], Mb[d]).then_inc(m0f.sem, 1)
                    act.wait_ge(m0f.sem, m0f.next(h))
                for d in range(2):
                    act.wait_ge(rf.sem, rf.at(h, 8 * u + d + 1))
                    act.copy(halves(Xb[d]), two_banks(4 * d)).then_inc(rev.sem, 1)
                    act.wait_ge(rev.sem, rev.next(h))
                for d in range(2):
                    act.wait_ge(m1.sem, m1.at(h, 4 * u + 2 * d + 2))
                    act.copy(MTb[d], MT[d]).then_inc(mtb.sem, 1)
                    act.wait_ge(mtb.sem, mtb.next(h))
                    act.wait_ge(rf.sem, rf.at(h, 8 * u + 4 + d + 1))
                    act.copy(halves(Xb[d]), two_banks(4 * d + 2)).then_inc(rev.sem, 1)
                    act.wait_ge(rev.sem, rev.next(h))
                for s_ in range(NT):
                    for d in range(2):
                        c = chunk(d, s_)
                        act.wait_ge(rv.sem, rv.at(h, 2 * (u * NT + s_) + d + 1))
                        act.wait_ge(ro.sem, ro.at(h, 2 * (u * NT + s_) + d + 1 - 2))
                        act.activation(v.V[:, d], ps[:, 4 * d + 1, 0:P], ACT.Copy,
                                       scale=sc_col(B, c, u, d)).then_inc(rve.sem, 1)
                        act.wait_ge(rve.sem, rve.next(h))
                act.wait_ge(osum.sem, osum.at(h, u + 1))
                for b, (t0, t1) in enumerate(PARTS):
                    act.activation(v.sq[:, t0:t1], ps[:, b, 0:t1 - t0], ACT.Ln, scale=1.0 / P,
                                   bias=env.epsc[:, 0:1]).then_inc(ors.sem, 1)
                    act.wait_ge(ors.sem, ors.next(h))
                act.activation(v.sq, v.sq, ACT.Exp, scale=-0.5).then_inc(ors.sem, 1)
                act.wait_ge(ors.sem, ors.next(h))

    def sc_col(kind, c, u, d):
        i = kind * NT + c
        return v.sch[:, i, 2 * d + u:2 * d + u + 1]

    def vector(dve):
        ps = env.ps
        tabv = v.table.rearrange("p (k c) n -> p k c n", k=KINDS)
        big = flat(v.MF[0])
        Z, A1, E1, L1 = (big[:, i * 192:(i + 1) * 192] for i in range(4))
        tok = lambda x, w=32: x.rearrange("p (c n) -> p c n", n=w)
        dve.wait_ge(t_mm.sem, t_mm.at(0, 1))
        dve.wait_ge(t_ld.sem, t_ld.at(0))
        pa = tok(ps[:, 0, 0:384], 64)[:, :, 0:32]
        dve.tensor_tensor(tok(Z), pa, dtrow.unsqueeze(1).broadcast_to([P, NT, 32]), ALU.add).then_inc(t_dve.sem, 1)
        dve.wait_ge(t_dve.sem, t_dve.next(0))
        dve.scalar_tensor_tensor(A1, Z, -1.0, Z, ALU.mult, ALU.max).then_inc(t_dve.sem, 1)
        dve.wait_ge(t_dve.sem, t_dve.next(0))
        dve.tensor_scalar(Z, Z, 0.0, None, ALU.max).then_inc(t_dve.sem, 1)
        dve.wait_ge(t_dve.sem, t_dve.next(0))
        dve.wait_ge(t_act.sem, t_act.at(0, 4))
        dve.tensor_tensor(Z, Z, L1, ALU.add).then_inc(t_dve.sem, 1)
        dve.wait_ge(t_dve.sem, t_dve.next(0))
        dve.scalar_tensor_tensor(tok(Z), tok(Z), -1.0, nega.unsqueeze(1).broadcast_to([P, NT, 32]),
                                 ALU.mult, ALU.mult).then_inc(t_dve.sem, 1)
        dve.wait_ge(t_dve.sem, t_dve.next(0))
        dve.tensor_copy(tabv[:, G], tok(Z)).then_inc(t_dve.sem, 1)
        dve.wait_ge(t_dve.sem, t_dve.next(0))
        dve.tensor_scalar(tabv[:, B], tabv[:, B], 1.0, None, ALU.add).then_inc(t_dve.sem, 1)
        dve.wait_ge(t_dve.sem, t_dve.next(0))
        dve.reciprocal(tabv[:, B], tabv[:, B]).then_inc(t_dve.sem, 1)
        dve.wait_ge(t_dve.sem, t_dve.next(0))
        dve.tensor_scalar(tabv[:, NB], tabv[:, B], -1.0, None, ALU.mult).then_inc(t_dve.sem, 1)
        dve.wait_ge(t_dve.sem, t_dve.next(0))
        dve.wait_ge(t_mm.sem, t_mm.at(0, 2))
        for d in range(2):
            dve.tensor_scalar(tabv[:, NGC, :, 16 * d:16 * d + 16],
                              tok(ps[:, 1 + d, 0:96], 16), -1.0, None, ALU.mult).then_inc(t_dve.sem, 1)
            dve.wait_ge(t_dve.sem, t_dve.next(0))
        dve.tensor_tensor(tabv[:, KDEC], tok(ps[:, 3, 0:192]), tabv[:, NGC], ALU.add).then_inc(t_dve.sem, 1)
        dve.wait_ge(t_dve.sem, t_dve.next(0))
        dve.wait_ge(t_act.sem, t_act.at(0))
        dve.memset(v.pad, 0.0).then_inc(t_dve.sem, 1)
        dve.wait_ge(t_dve.sem, t_dve.next(0))
        dve.memset(Xb[0], 0.0).then_inc(t_dve.sem, 1)
        dve.wait_ge(t_dve.sem, t_dve.next(0))
        dve.memset(Xb[1], 0.0).then_inc(t_dve.sem, 1)
        dve.wait_ge(t_dve.sem, t_dve.next(0))
        dve.tensor_scalar(v.offdiag, env.ident, -1.0, 1.0, ALU.mult, ALU.add).then_inc(t_dve.sem, 1)
        dve.wait_ge(t_dve.sem, t_dve.next(0))

        with dve.Fori(0, GH) as h:
            for n in range(4):
                dve.wait_ge(padw.sem, padw.at(h, 2 * n + 2))
                dve.wait_ge(silu.sem, silu.at(h, 2 * (n - 1)))
                if n == 0:
                    dve.wait_ge(stage.sem, stage.at(h))
                tile_i = (0, 1, 2, 3)[n]
                conv(dve, v.acc[:, n % 2], v.pad[:, n % 2], lambda w_: v.cw[:, w_, tile_i:tile_i + 1], convd, h)
                if n == 2:
                    for i in range(2):
                        dve.wait_ge(rsd.sem, rsd.at(h, 3 * i + 3))
                        t = v.k if i == 0 else v.q
                        dve.tensor_tensor(t, t, v.sq if i == 0 else v.gt, ALU.mult).then_inc(nrm.sem, 1)
                        dve.wait_ge(nrm.sem, nrm.next(h))
            dve.wait_ge(tev.sem, tev.at(h, 4))
            dve.tensor_tensor(v.KK, v.KK, v.offdiag.unsqueeze(1).broadcast_to([P, NT, P]), ALU.mult).then_inc(strict.sem, 1)
            dve.wait_ge(strict.sem, strict.next(h))
            for u in range(2):
                for d in range(2):
                    dve.wait_ge(egd.sem, egd.at(h, 2 * u + d + 1))
                    dve.wait_ge(rf.sem, rf.at(h, 8 * u))
                    cap = env.cap_f if d == 0 else env.cap_b
                    for c in range(NT):
                        src = ps[:, 2 * d + c // 3, (c % 3) * P:(c % 3 + 1) * P]
                        dve.scalar_tensor_tensor(DEC[d][:, c], src, sc_col(NGC, c, u, d), cap,
                                                 ALU.add, ALU.min).then_inc(dmat.sem, 1)
                        dve.wait_ge(dmat.sem, dmat.next(h))
                for d in range(2):
                    dve.wait_ge(decd.sem, decd.at(h, 2 * u + d + 1))
                    for c in range(NT):
                        dve.scalar_tensor_tensor(NAT[d][:, c], v.KK[:, c], sc_col(NB, c, u, d),
                                                 DEC[d][:, c], ALU.mult, ALU.mult).then_inc(natd.sem, 1)
                        dve.wait_ge(natd.sem, natd.next(h))
                two_banks = lambda b0: ps[:, b0:b0 + 2, 0:384]
                halves = lambda t: t.rearrange("p (i c) n -> p i (c n)", i=2)
                for lv in range(LEVELS):
                    s = 1 << lv
                    for d in range(2):
                        g = 2 * u + d
                        mask_m = env.m4[:, d, lv].rearrange("p (b s) -> p b s", s=s).unsqueeze(1).broadcast_to([P, NT, 64 // s, s])
                        mask_t = env.m4[:, 1 - d, lv].rearrange("p (b s) -> p b s", s=s).unsqueeze(1).broadcast_to([P, NT, 64 // s, s])
                        bank = lambda b: ps[:, b, 0:384].rearrange("p (c b s) -> p c b s", c=NT, s=s)
                        if lv == 0:
                            dve.wait_ge(inx.sem, inx.at(h, 2 * u * LEVELS + d + 1))
                            dve.wait_ge(minit.sem, minit.at(h, 4 * u + 2 * d + 2))
                            dve.wait_ge(natb.sem, natb.at(h, g + 1))
                            src_m, src_t = bank(4 * d), half_cols(NATb[d], s, 1 - d)
                        else:
                            dve.wait_ge(iny.sem, iny.at(h, 2 * (u * (LEVELS - 1) + lv - 1) + d + 1))
                            src_m, src_t = bank(4 * d + 1), bank(4 * d + 2)
                        hold(env, dve)
                        dve.copy_predicated(half_cols(Mb[d], s, d), mask_m, src_m).then_inc(inm.sem, 1)
                        dve.wait_ge(inm.sem, inm.next(h))
                        hold(env, dve)
                        dve.copy_predicated(half_cols(MTb[d], s, 1 - d), mask_t, src_t).then_inc(inm.sem, 1)
                        dve.wait_ge(inm.sem, inm.next(h))
                for d in range(2):
                    if u == 0:
                        dve.wait_ge(tev.sem, tev.at(h, 6))
                    dve.tensor_tensor(QKD[d], DEC[d], v.QK, ALU.mult).then_inc(qkd.sem, 1)
                    dve.wait_ge(qkd.sem, qkd.next(h))
                for d in range(2):
                    dve.wait_ge(rf.sem, rf.at(h, 8 * u + 2 + d + 1))
                    dve.tensor_tensor(halves(MF[d]), halves(MF[d]), two_banks(4 * d + 2), ALU.add).then_inc(m1.sem, 1)
                    dve.wait_ge(m1.sem, m1.next(h))
                    dve.tensor_tensor(halves(MT[d]), halves(MTb[d]), two_banks(4 * d), ALU.add).then_inc(m1.sem, 1)
                    dve.wait_ge(m1.sem, m1.next(h))
                for d in range(2):
                    dve.wait_ge(rf.sem, rf.at(h, 8 * u + 6 + d + 1))
                    dve.tensor_tensor(halves(MT[d]), halves(MT[d]), two_banks(4 * d), ALU.add).then_inc(mtf.sem, 1)
                    dve.wait_ge(mtf.sem, mtf.next(h))
                for s_ in range(NT):
                    r = 10 * u + 2 * (s_ - 1)
                    for d in range(2):
                        c = chunk(d, s_)
                        if s_ > 0:
                            dve.wait_ge(rks.sem, rks.at(h, r + d + 1))
                            dve.wait_ge(rv.sem, rv.at(h, 12 * u + 2 * s_ + d + 1 - 2))
                            dve.scalar_tensor_tensor(v.R[:, d], ps[:, 4 * d, 0:P], sc_col(NEG, c, u, d),
                                                     v.vtok[:, u, c], ALU.mult, ALU.add).then_inc(rr.sem, 1)
                            dve.wait_ge(rr.sem, rr.next(h))
                    for d in range(2):
                        c = chunk(d, s_)
                        dve.wait_ge(ro.sem, ro.at(h, 12 * u + 2 * s_ + d + 1))
                        if s_ < NT - 1:
                            if s_ == 0:
                                dve.tensor_copy(v.S[:, d], ps[:, 4 * d + 2, 0:P]).then_inc(rue.sem, 1)
                                dve.wait_ge(rue.sem, rue.next(h))
                            else:
                                dve.scalar_tensor_tensor(v.S[:, d], v.S[:, d], sc_col(DCH, c, u, d),
                                                         ps[:, 4 * d + 2, 0:P], ALU.mult, ALU.add).then_inc(rue.sem, 1)
                                dve.wait_ge(rue.sem, rue.next(h))
                        ot = v.OT[:, c * P:(c + 1) * P]
                        if first_seen[c] == (s_, d):
                            dve.tensor_copy(ot, ps[:, 4 * d + 3, 0:P]).then_inc(roe.sem, 1)
                            dve.wait_ge(roe.sem, roe.next(h))
                        else:
                            dve.tensor_tensor(ot, ot, ps[:, 4 * d + 3, 0:P], ALU.add).then_inc(roe.sem, 1)
                            dve.wait_ge(roe.sem, roe.next(h))
                dve.wait_ge(ors.sem, ors.at(h, 3 * u + 3))
                dve.wait_ge(st.sem, st.at(h, u))
                dve.scalar_tensor_tensor(v.gt, v.OT, env.vec[:, 1, GN_ROW + j:GN_ROW + j + 1], v.sq,
                                         ALU.mult, ALU.mult).then_inc(og.sem, 1)
                dve.wait_ge(og.sem, og.next(h))
                dve.tensor_tensor(v.gt, v.gt, v.sz[:, u], ALU.mult).then_inc(og.sem, 1)
                dve.wait_ge(og.sem, og.next(h))

    def gpsimd(pool):
        pool.wait_ge(t_dve.sem, t_dve.at(0))
        pool.wait_ge(t_act.sem, t_act.at(0))
        convt = env.vec[:, 2 + j, :].rearrange("p (w t) -> p w t", w=4)
        with pool.Fori(0, GH) as h:
            pool.wait_ge(convd.sem, convd.at(h, 0))
            pool.wait_ge(og.sem, og.at(h, 0))
            pool.wait_ge(rve.sem, rve.at(h, 0))
            hold(env, pool)
            pool.tensor_copy(v.cw[:, :, 0:1], convt[:, :, ds(h + 8, 1)]).then_inc(stage.sem, 1)
            pool.wait_ge(stage.sem, stage.next(h))
            hold(env, pool)
            pool.tensor_copy(v.cw[:, :, 1:2], convt[:, :, ds(h, 1)]).then_inc(stage.sem, 1)
            pool.wait_ge(stage.sem, stage.next(h))
            hold(env, pool)
            pool.tensor_copy(v.cw[:, :, 2:4], convt[:, :, ds(2 * h + 16, 2)]).then_inc(stage.sem, 1)
            pool.wait_ge(stage.sem, stage.next(h))
            hold(env, pool)
            pool.tensor_copy(v.sch.rearrange("p i (d u) -> p i d u", d=2),
                             v.table.rearrange("p i (d n) -> p i d n", d=2)[:, :, :, ds(2 * h, 2)]).then_inc(stage.sem, 1)
            pool.wait_ge(stage.sem, stage.next(h))
            for i, (t, buf) in enumerate(((v.k, v.sq), (v.q, v.gt))):
                pool.wait_ge(silu.sem, silu.at(h, 2 * i + 2))
                if i == 1:
                    pool.wait_ge(st.sem, st.at(h, 0))
                pool.tensor_tensor(buf, t, t, ALU.mult).then_inc(sqd.sem, 1)
                pool.wait_ge(sqd.sem, sqd.next(h))

            def summands(u):
                pool.wait_ge(rf.sem, rf.at(h, 8 * u))
                for d in range(2):
                    tri = (env.upper, env.lower)[d]
                    col = v.sch[:, G * NT:(G + 1) * NT, 2 * d + u:2 * d + u + 1].broadcast_to([P, NT, P])
                    pool.tensor_tensor(MF[d], tri.unsqueeze(1).broadcast_to([P, NT, P]), col, ALU.mult).then_inc(ugd.sem, 1)
                    pool.wait_ge(ugd.sem, ugd.next(h))

            summands(0)
            for u in range(2):
                for d in range(2):
                    g = 2 * u + d
                    pool.wait_ge(natb.sem, natb.at(h, g + 1))
                    idb = env.ident.unsqueeze(1).broadcast_to([P, NT, P])
                    pool.tensor_tensor(NAT[d], NAT[d], idb, ALU.subtract).then_inc(nati.sem, 1)
                    pool.wait_ge(nati.sem, nati.next(h))
                pool.wait_ge(nrm.sem, nrm.at(h))
                for d in range(2):
                    pool.wait_ge(egd.sem, egd.at(h, 2 * u + d + 1))
                    pool.tensor_tensor(flat(QD[d]), flat(QD[d]), v.q, ALU.mult).then_inc(qdd.sem, 1)
                    pool.wait_ge(qdd.sem, qdd.next(h))
                pool.wait_ge(tev.sem, tev.at(h, 2))
                pool.wait_ge(ru.sem, ru.at(h, 10 * u))
                for d in range(2):
                    for c in range(NT):
                        hold(env, pool)
                        pool.tensor_scalar(KDX[d][:, c], v.ktok[:, c], sc_col(KDEC, c, u, d), None, ALU.mult).then_inc(kdec.sem, 1)
                        pool.wait_ge(kdec.sem, kdec.next(h))
                if u == 0:
                    summands(1)
                pool.wait_ge(roe.sem, roe.at(h, 12 * (u + 1)))
                pool.wait_ge(og.sem, og.at(h, 2 * u))
                pool.tensor_tensor(v.sq, v.OT, v.OT, ALU.mult).then_inc(osq.sem, 1)
                pool.wait_ge(osq.sem, osq.next(h))

    return dict(sync=sync, tensor=tensor, scalar=scalar, vector=vector, gpsimd=gpsimd)




def lru_phase(env, l):
    a = env.a
    j = 0
    v = carve(env, [("pad", (PADW,)), ("acc", (CONVW,)), ("u", (T,)), ("sg", (T,)), ("cw", (12,)), ("lam", (6, 16)),
                    ("gt", (T,)), ("h0", (T,)), ("h1", (T,)),
                    ("r", (2, T)), ("i", (2, T)), ("sq", (2, T)), ("rc", (2, T)), ("a", (2, T)), ("gw", (4, P))])
    S = lambda n, per=1, step=1: Sig(env, "lru_" + n, per, step, LRU_N)
    w_ld = [S(f"w_ld{i}", (1, 1, 4)[i], 16) for i in range(3)]
    lamd = Sig(env, "lru_lam_dve", 15)
    lama = Sig(env, "lru_lam_act", 1)
    stage = S("stage", 3)
    proj = S("proj", 2)
    padw = S("padw", 2)
    convd = S("convd", 4)
    ucp = S("ucp", 2)
    sgd = S("sgd", 2)
    gates = S("gates", 4)
    gact = S("gact", 10)
    sqr = S("sqr", 2)
    rcd = S("rcd", 6)
    iu = S("iu", 2)
    bd = S("bd", 4)
    scn = S("scn", 3)
    og = S("og", 2)
    st = S("st", 1, 16)
    U0 = D
    w_in = a["lru_w_in"][j].rearrange("(k p) n -> p k n", p=P)
    gw = [a[n][j].rearrange("d n c e -> n d c e") for n in ("lru_w_ra", "lru_w_ri")]

    def sync(sp):
        def load(i, h):
            if i < 2:
                sp.dma_start(env.W[:, i], w_in[:, :, ds(h * P + (U0 if i == 0 else 0), P)]).then_inc(w_ld[i].sem, 16)
            else:
                for d in range(2):
                    for g in range(2):
                        sp.dma_start(v.gw[:, 2 * d + g], gw[g][ds(h, 1), d].rearrange("o c e -> (o c) e")).then_inc(w_ld[2].sem, 16)

        def store(h):
            sp.wait_ge(og.sem, og.at(h))
            sp.dma_start(a["scratch"][ds(h, 1)].rearrange("o p t -> (o p) t"), v.gt).then_inc(st.sem, 16)

        for i in range(3):
            load(i, 0)
        with sp.Fori(0, LRU_N - 1) as h:
            for i, (sig, k) in enumerate(((proj, 1), (proj, 2), (gates, 4))):
                sp.wait_ge(sig.sem, sig.at(h, k))
                hold(env, sp)
                load(i, h + 1)
            store(h)
        store(LRU_N - 1)
        sp.wait_ge(st.sem, st.at(LRU_N - 1))

    def tensor(pe):
        pe.wait_ge(lamd.sem, lamd.at(0))
        with pe.Fori(0, LRU_N) as h:
            pe.wait_ge(w_ld[0].sem, w_ld[0].at(h))
            pe.wait_ge(gact.sem, gact.at(h, 0))
            project(pe, env, 0, (0, 1)).then_inc(proj.sem, 1)
            pe.wait_ge(w_ld[1].sem, w_ld[1].at(h))
            project(pe, env, 1, (2, 3)).then_inc(proj.sem, 1)
            pe.wait_ge(w_ld[2].sem, w_ld[2].at(h))
            pe.wait_ge(ucp.sem, ucp.at(h))
            pe.wait_ge(padw.sem, padw.at(h))
            for g in range(4):
                if g == 3:
                    pe.wait_ge(sgd.sem, sgd.at(h))
                for b, (t0, t1) in enumerate(PARTS):
                    mm = pe.matmul(env.ps[:, (4, 6, 0, 2)[g] + b, 0:t1 - t0], v.gw[:, g], v.u[:, t0:t1], start=True, stop=True)
                mm.then_inc(gates.sem, 1)

    def scalar(act):
        ps = env.ps
        act.wait_ge(lamd.sem, lamd.at(0, 3))
        hold(env, act)
        act.preload_act_table_set(LNEXP)
        act.activation(v.lam[:, 1], v.lam[:, 1], ACT.Exp, scale=-1.0).then_inc(lama.sem, 1)
        act.wait_ge(lama.sem, lama.next(0))
        with act.Fori(0, LRU_N) as h:
            act.wait_ge(proj.sem, proj.at(h, 1))
            act.wait_ge(convd.sem, convd.at(h, 0))
            for i, (t0, t1) in enumerate(PARTS):
                act.copy(v.pad[:, PAD_AT[i]:PAD_AT[i] + t1 - t0], ps[:, i, 0:t1 - t0]).then_inc(padw.sem, 1)
                act.wait_ge(padw.sem, padw.next(h))
            act.wait_ge(og.sem, og.at(h, 0))
            act.wait_ge(proj.sem, proj.at(h, 2))
            for i, (t0, t1) in enumerate(PARTS):
                act.activation(v.sg[:, t0:t1], ps[:, 2 + i, 0:t1 - t0], ACT.Silu).then_inc(sgd.sem, 1)
                act.wait_ge(sgd.sem, sgd.next(h))
            act.wait_ge(convd.sem, convd.at(h))
            act.wait_ge(iu.sem, iu.at(h, 0))
            act.wait_ge(gates.sem, gates.at(h, 0))
            for i, (t0, t1) in enumerate(PARTS):
                act.copy(v.u[:, t0:t1], v.acc[:, t0 + 2 * i:t1 + 2 * i]).then_inc(ucp.sem, 1)
                act.wait_ge(ucp.sem, ucp.next(h))
            act.wait_ge(stage.sem, stage.at(h))
            act.wait_ge(rcd.sem, rcd.at(h, 0))
            act.wait_ge(bd.sem, bd.at(h, 0))
            for d in range(2):
                for g in range(2):
                    act.wait_ge(gates.sem, gates.at(h, 2 * d + g + 1))
                    for i, (t0, t1) in enumerate(PARTS):
                        act.activation((v.r, v.i)[g][:, d, t0:t1], ps[:, (4, 6, 0, 2)[2 * d + g] + i, 0:t1 - t0],
                                       ACT.Sigmoid, bias=v.cw[:, 5 + 2 * d + g:6 + 2 * d + g]).then_inc(gact.sem, 1)
                        act.wait_ge(gact.sem, gact.next(h))
                act.activation(v.r[:, d], v.r[:, d], ACT.Tanh, scale=v.cw[:, 9 + d:10 + d]).then_inc(gact.sem, 1)
                act.wait_ge(gact.sem, gact.next(h))
            for d in range(2):
                act.activation(v.sq[:, d], v.r[:, d], ACT.Sqrt, scale=-4.0).then_inc(sqr.sem, 1)
                act.wait_ge(sqr.sem, sqr.next(h))

    def vector(dve):
        lam = env.vec[:, 1, LAM_ROW:LAM_ROW + 16]
        dve.memset(v.pad, 0.0).then_inc(lamd.sem, 1)
        dve.wait_ge(lamd.sem, lamd.next(0))
        dve.tensor_scalar(v.lam[:, 0], lam, -1.0, 0.0, ALU.mult, ALU.max).then_inc(lamd.sem, 1)
        dve.wait_ge(lamd.sem, lamd.next(0))
        dve.scalar_tensor_tensor(v.lam[:, 1], lam, -1.0, lam, ALU.mult, ALU.max).then_inc(lamd.sem, 1)
        dve.wait_ge(lamd.sem, lamd.next(0))
        dve.wait_ge(lama.sem, lama.at(0))
        dve.tensor_scalar(v.lam[:, 2], v.lam[:, 1], 2.0, None, ALU.add).then_inc(lamd.sem, 1)
        dve.wait_ge(lamd.sem, lamd.next(0))
        dve.reciprocal(v.lam[:, 2], v.lam[:, 2]).then_inc(lamd.sem, 1)
        dve.wait_ge(lamd.sem, lamd.next(0))
        dve.tensor_tensor(v.lam[:, 3], v.lam[:, 1], v.lam[:, 2], ALU.mult).then_inc(lamd.sem, 1)
        dve.wait_ge(lamd.sem, lamd.next(0))
        dve.tensor_tensor(v.lam[:, 4], v.lam[:, 3], v.lam[:, 3], ALU.mult).then_inc(lamd.sem, 1)
        dve.wait_ge(lamd.sem, lamd.next(0))
        dve.tensor_scalar(v.lam[:, 5], v.lam[:, 4], 1.0 / 11, None, ALU.mult).then_inc(lamd.sem, 1)
        dve.wait_ge(lamd.sem, lamd.next(0))
        for c in (9, 7, 5, 3):
            dve.scalar_tensor_tensor(v.lam[:, 5], v.lam[:, 5], 1.0 / c, v.lam[:, 4], ALU.add, ALU.mult).then_inc(lamd.sem, 1)
            dve.wait_ge(lamd.sem, lamd.next(0))
        dve.scalar_tensor_tensor(v.lam[:, 5], v.lam[:, 5], 1.0, v.lam[:, 3], ALU.add, ALU.mult).then_inc(lamd.sem, 1)
        dve.wait_ge(lamd.sem, lamd.next(0))
        dve.scalar_tensor_tensor(v.lam[:, 5], v.lam[:, 5], 2.0, v.lam[:, 0], ALU.mult, ALU.add).then_inc(lamd.sem, 1)
        dve.wait_ge(lamd.sem, lamd.next(0))
        dve.tensor_scalar(v.lam[:, 5], v.lam[:, 5], -4.0, None, ALU.mult).then_inc(lamd.sem, 1)
        dve.wait_ge(lamd.sem, lamd.next(0))
        with dve.Fori(0, LRU_N) as h:
            dve.wait_ge(padw.sem, padw.at(h))
            dve.wait_ge(stage.sem, stage.at(h))
            dve.wait_ge(ucp.sem, ucp.at(h, 0))
            dve.tensor_scalar(v.acc, v.pad[:, 0:CONVW], v.cw[:, 0:1], v.cw[:, 4:5], ALU.mult, ALU.add).then_inc(convd.sem, 1)
            dve.wait_ge(convd.sem, convd.next(h))
            for w_ in range(1, 4):
                dve.scalar_tensor_tensor(v.acc, v.pad[:, w_:w_ + CONVW], v.cw[:, w_:w_ + 1], v.acc,
                                         ALU.mult, ALU.add).then_inc(convd.sem, 1)
                dve.wait_ge(convd.sem, convd.next(h))
            for d in range(2):
                dve.wait_ge(gact.sem, gact.at(h, 5 * d + 5))
                dve.tensor_scalar(v.rc[:, d], v.r[:, d], -1.0, 1.0, ALU.mult, ALU.add).then_inc(rcd.sem, 1)
                dve.wait_ge(rcd.sem, rcd.next(h))
                dve.reciprocal(v.rc[:, d], v.rc[:, d]).then_inc(rcd.sem, 1)
                dve.wait_ge(rcd.sem, rcd.next(h))
                dve.tensor_scalar(v.a[:, d], v.rc[:, d], 2.0, -1.0, ALU.mult, ALU.add).then_inc(rcd.sem, 1)
                dve.wait_ge(rcd.sem, rcd.next(h))
            for d in range(2):
                dve.wait_ge(sqr.sem, sqr.at(h, d + 1))
                dve.tensor_tensor(v.rc[:, d], v.rc[:, d], v.sq[:, d], ALU.mult).then_inc(bd.sem, 1)
                dve.wait_ge(bd.sem, bd.next(h))
                dve.wait_ge(iu.sem, iu.at(h, d + 1))
                dve.tensor_tensor(v.rc[:, d], v.rc[:, d], v.i[:, d], ALU.mult).then_inc(bd.sem, 1)
                dve.wait_ge(bd.sem, bd.next(h))
            dve.tensor_tensor_scan(v.h0, v.a[:, 0], v.rc[:, 0], 0.0, ALU.mult, ALU.add).then_inc(scn.sem, 1)
            dve.wait_ge(scn.sem, scn.next(h))
            rev = lambda x, t0, t1: x[:, t0:t1][:, ::-1]
            dve.tensor_tensor_scan(rev(v.h1, 0, CTX), rev(v.a[:, 1], 0, CTX), rev(v.rc[:, 1], 0, CTX), 0.0,
                                   ALU.mult, ALU.add).then_inc(scn.sem, 1)
            dve.wait_ge(scn.sem, scn.next(h))
            dve.tensor_tensor_scan(rev(v.h1, CTX, T), rev(v.a[:, 1], CTX, T), rev(v.rc[:, 1], CTX, T),
                                   v.h1[:, 0:1], ALU.mult, ALU.add).then_inc(scn.sem, 1)
            dve.wait_ge(scn.sem, scn.next(h))
            dve.tensor_tensor(v.h0, v.h0, v.h1, ALU.add).then_inc(og.sem, 1)
            dve.wait_ge(og.sem, og.next(h))
            dve.wait_ge(st.sem, st.at(h, 0))
            dve.wait_ge(sgd.sem, sgd.at(h))
            dve.tensor_tensor(v.gt, v.h0, v.sg, ALU.mult).then_inc(og.sem, 1)
            dve.wait_ge(og.sem, og.next(h))

    def gpsimd(pool):
        pool.wait_ge(lamd.sem, lamd.at(0))
        convt = env.vec[:, 4, 0:32].rearrange("p (w t) -> p w t", w=4)
        with pool.Fori(0, LRU_N) as h:
            pool.wait_ge(convd.sem, convd.at(h, 0))
            pool.wait_ge(gact.sem, gact.at(h, 0))
            hold(env, pool)
            pool.tensor_copy(v.cw[:, 0:4].unsqueeze(2), convt[:, :, ds(h, 1)]).then_inc(stage.sem, 1)
            pool.wait_ge(stage.sem, stage.next(h))
            hold(env, pool)
            pool.tensor_copy(v.cw[:, 4:5], env.vec[:, 0, CB_ROW:CB_ROW + 8][:, ds(h, 1)]).then_inc(stage.sem, 1)
            pool.wait_ge(stage.sem, stage.next(h))
            bias = env.vec[:, 0, BRA_ROW:BRA_ROW + 32].rearrange("p (g d n) -> p d g n", g=2, d=2)
            hold(env, pool)
            pool.tensor_copy(v.cw[:, 5:9].rearrange("p (d g) -> p d g", d=2).unsqueeze(3), bias[:, :, :, ds(h, 1)])
            hold(env, pool)
            pool.tensor_copy(v.cw[:, 9:11].unsqueeze(2), v.lam[:, 5].rearrange("p (d n) -> p d n", d=2)[:, :, ds(h, 1)]).then_inc(stage.sem, 1)
            pool.wait_ge(stage.sem, stage.next(h))
            for d in range(2):
                pool.wait_ge(gact.sem, gact.at(h, 5 * d + 5))
                pool.wait_ge(ucp.sem, ucp.at(h))
                pool.tensor_tensor(v.i[:, d], v.i[:, d], v.u, ALU.mult).then_inc(iu.sem, 1)
                pool.wait_ge(iu.sem, iu.next(h))

    return dict(sync=sync, tensor=tensor, scalar=scalar, vector=vector, gpsimd=gpsimd)


def att_phase(env, l):
    a = env.a
    j = 0
    SC = AHD ** -0.5
    v = carve(env, [("q", (2, T)), ("k", (T,)), ("sz", (2, T)), ("rot", (SEQ,)), ("vt", (NT, AHD)), ("gt", (2, T)),
                    ("sk", (16,)), ("skh", (4,)), ("mx", (2, 4)), ("s", (2, 640)), ("pt", (2, 640)),
                    ("wv", (KD, AHD)), ("wk", (KD, P))])
    S = lambda n, per=1, step=1: Sig(env, "att_" + n, per, step, AKV)
    w_ld = [S(f"w_ld{i}", (2, 2, 2, 1)[i], 16) for i in range(4)]
    skl = Sig(env, "att_sink_ld", 1, 16)
    stage = S("stage", 1)
    proj = S("proj", 6)
    zev = S("zev", 4)
    qev = S("qev", 7)
    perm = S("perm", 3)
    rsin = S("rsin", 3)
    rcos = S("rcos", 3)
    radd = S("radd", 3)
    NU = AGRP * NT
    sc = S("sc", NU)
    sm = S("sm", 4 * NU + 8)
    ex = S("ex", 2 * NU)
    pn = S("pn", 3 * NU)
    tp = S("tp", NU)
    te = S("te", NU)
    pv = S("pv", NU)
    og = S("og", NU)
    st = S("st", 1, 16)
    w_in = a["att_w_in"][j].rearrange("(k p) n -> p k n", p=P)
    QC, KC, VC, ZC = 0, 1024, 1280, 1536
    units = [(r, t) for r in range(AGRP) for t in range(NT)]

    def window(t):
        if t < CT:
            return None
        return max(t - 1, CT), min(t + 1, NT - 1)

    def blocks(t):
        w = window(t)
        return list(range(CT)) + (list(range(w[0], w[1] + 1)) if w else [])

    def sync(sp):
        sp.dma_start(v.sk, flat_dram(a["att_sinks"][j]).partition_broadcast(P)).then_inc(skl.sem, 16)

        def load(i, h):
            if i < 2:
                for u in range(2):
                    sp.dma_start(env.W[:, 2 * i + u], w_in[:, :, ds(h * 256 + (ZC, QC)[i] + u * P, P)]).then_inc(w_ld[i].sem, 16)
            elif i == 2:
                for u in range(2):
                    sp.dma_start(v.wk[:, :, u * AHD:(u + 1) * AHD], w_in[:, :, ds(h * AHD + KC, AHD)]).then_inc(w_ld[i].sem, 16)
            else:
                sp.dma_start(v.wv, w_in[:, :, ds(h * AHD + VC, AHD)]).then_inc(w_ld[i].sem, 16)

        def store(h):
            sp.wait_ge(og.sem, og.at(h))
            sp.dma_start(a["scratch"].rearrange("(g u) p t -> g p u t", u=2)[ds(h, 1)].rearrange("o p u t -> (o p) u t"),
                         v.gt).then_inc(st.sem, 16)

        for i in range(4):
            load(i, 0)
        with sp.Fori(0, AKV - 1) as h:
            for i, n in enumerate((2, 4, 5, 6)):
                sp.wait_ge(proj.sem, proj.at(h, n))
                hold(env, sp)
                load(i, h + 1)
            store(h)
        store(AKV - 1)
        sp.wait_ge(st.sem, st.at(AKV - 1))

    def tensor(pe):
        ps = env.ps
        with pe.Fori(0, AKV) as h:
            pe.wait_ge(og.sem, og.at(h, 0))
            pe.wait_ge(te.sem, te.at(h, 0))
            for n in range(2):
                if n == 0:
                    pe.wait_ge(w_ld[0].sem, w_ld[0].at(h))
                project(pe, env, n, (2 * n, 2 * n + 1)).then_inc(proj.sem, 1)
            pe.wait_ge(w_ld[1].sem, w_ld[1].at(h))
            for n in range(2):
                if n == 1:
                    pass
                project(pe, env, 2 + n, (4 + 2 * n, 5 + 2 * n)).then_inc(proj.sem, 1)
            pe.wait_ge(w_ld[2].sem, w_ld[2].at(h))
            pe.wait_ge(zev.sem, zev.at(h, 2))
            for b, (t0, t1) in enumerate(PARTS):
                for k in range(KD):
                    mm = pe.matmul(ps[:, b, 0:t1 - t0], v.wk[:, k, :], env.hT[:, k, t0:t1], start=(k == 0), stop=(k == KD - 1))
            mm.then_inc(proj.sem, 1)
            pe.wait_ge(w_ld[3].sem, w_ld[3].at(h))
            pe.wait_ge(zev.sem, zev.at(h, 4))
            for t in range(NT):
                for k in range(KD):
                    mm = pe.matmul(ps[:, 2, t * AHD:(t + 1) * AHD], env.hT[:, k, t * P:(t + 1) * P], v.wv[:, k, :],
                                   start=(k == 0), stop=(k == KD - 1))
            mm.then_inc(proj.sem, 1)
            for n, (src, need) in enumerate(((v.q[:, 0], 2), (v.q[:, 1], 4), (v.k, 6))):
                pe.wait_ge(qev.sem, qev.at(h, need))
                b = (3, 4, 5)[n]
                pe.matmul(ps[:, b, 0:SEQ], env.perm, src[:, CTX:T], start=True, stop=True).then_inc(perm.sem, 1)
            pe.wait_ge(radd.sem, radd.at(h))
            pe.wait_ge(qev.sem, qev.at(h))

            def scores(n):
                r, t = units[n]
                pb = (r % 2) * AHD
                q = v.q[pb:pb + AHD, r // 2, t * P:(t + 1) * P]
                b = 2 * (n % 2)
                if n >= 2:
                    pe.wait_ge(sm.sem, sm.at(h, sm_at(n - 2, 2)))
                mm = pe.matmul(ps[:, b, 0:CTX], q, v.k[pb:pb + AHD, 0:CTX], start=True, stop=True)
                if window(t):
                    lo, hi = window(t)
                    mm = pe.matmul(ps[:, b + 1, 0:(hi + 1 - lo) * P], q, v.k[pb:pb + AHD, lo * P:(hi + 1) * P],
                                   start=True, stop=True)
                mm.then_inc(sc.sem, 1)

            def transposes(n):
                pe.wait_ge(pn.sem, pn.at(h, 3 * n + 3))
                if n >= 1:
                    pe.wait_ge(te.sem, te.at(h, n))
                for i in range(len(blocks(units[n][1]))):
                    mm = pe.transpose(ps[:, 4 + i // 4, (i % 4) * P:(i % 4 + 1) * P], v.s[:, n % 2, i * P:(i + 1) * P], env.ident)
                mm.then_inc(tp.sem, 1)

            def values(n):
                r, t = units[n]
                pb = (r % 2) * AHD
                pe.wait_ge(te.sem, te.at(h, n + 1))
                if n >= 2:
                    pe.wait_ge(og.sem, og.at(h, n - 1))
                bl = blocks(t)
                for i, kt in enumerate(bl):
                    mm = pe.matmul(ps[pb:pb + AHD, 6 + n % 2, 0:P], v.vt[:, kt, :], v.pt[:, n % 2, i * P:(i + 1) * P],
                                   start=(i == 0), stop=(i == len(bl) - 1))
                mm.then_inc(pv.sem, 1)

            for n in range(NU + 2):
                if n < NU:
                    scores(n)
                if 1 <= n <= NU:
                    transposes(n - 1)
                if n >= 2:
                    values(n - 2)

    def sm_at(n, upto):
        k = 0
        for m in range(n):
            k += 3 if units[m][1] < CT else 4
        if units[n][1] < CT:
            return k + (1 if upto == 2 else 3)
        return k + upto

    def scalar(act):
        ps = env.ps
        act.wait_ge(skl.sem, skl.at(0))
        with act.Fori(0, AKV) as h:
            act.wait_ge(og.sem, og.at(h, 0))
            for u in range(2):
                act.wait_ge(proj.sem, proj.at(h, u + 1))
                for i, (t0, t1) in enumerate(PARTS):
                    act.activation(v.sz[:, u, t0:t1], ps[:, 2 * u + i, 0:t1 - t0], ACT.Silu).then_inc(zev.sem, 1)
                    act.wait_ge(zev.sem, zev.next(h))
            act.wait_ge(sc.sem, sc.at(h, 0))
            act.wait_ge(pv.sem, pv.at(h, 0))
            for n, (dst, b) in enumerate(((v.q[:, 0], 4), (v.q[:, 1], 6), (v.k, 0))):
                act.wait_ge(proj.sem, proj.at(h, 3 + n))
                for i, (t0, t1) in enumerate(PARTS):
                    act.copy(dst[:, t0:t1], ps[:, b + i, 0:t1 - t0]).then_inc(qev.sem, 1)
                    act.wait_ge(qev.sem, qev.next(h))
            act.wait_ge(proj.sem, proj.at(h, 6))
            act.copy(v.vt, ps[:, 2, 0:NT * AHD].rearrange("p (t e) -> p t e", t=NT)).then_inc(qev.sem, 1)
            act.wait_ge(qev.sem, qev.next(h))

            def exps(n):
                r, t = units[n]
                w = len(blocks(t)) * P
                act.wait_ge(sm.sem, sm.at(h, sm_at(n, 4)))
                act.activation(v.s[:, n % 2, 0:w], v.s[:, n % 2, 0:w], ACT.Exp, bias=v.mx[:, n % 2, 0:1],
                               accum_out=v.mx[:, n % 2, 1:2]).then_inc(ex.sem, 1)
                act.wait_ge(ex.sem, ex.next(h))
                act.activation(v.mx[:, n % 2, 2:3], v.skh[:, r:r + 1], ACT.Exp, bias=v.mx[:, n % 2, 0:1]).then_inc(ex.sem, 1)
                act.wait_ge(ex.sem, ex.next(h))

            def keep(n):
                w = len(blocks(units[n][1])) * P
                act.wait_ge(tp.sem, tp.at(h, n + 1))
                act.wait_ge(pv.sem, pv.at(h, n - 1))
                act.copy(v.pt[:, n % 2, 0:w], ps[:, 4:6, :].rearrange("p a b -> p (a b)")[:, 0:w]).then_inc(te.sem, 1)
                act.wait_ge(te.sem, te.next(h))

            for n in range(NU + 1):
                if n < NU:
                    exps(n)
                if n >= 1:
                    keep(n - 1)

    def vector(dve):
        ps = env.ps
        with dve.Fori(0, AKV) as h:
            dve.wait_ge(stage.sem, stage.at(h))
            for n, (src, need) in enumerate(((v.q[:, 0], 2), (v.q[:, 1], 4), (v.k, 6))):
                dve.wait_ge(perm.sem, perm.at(h, n + 1))
                dve.tensor_tensor(v.rot, ps[:, (3, 4, 5)[n], 0:SEQ], env.sin, ALU.mult).then_inc(rsin.sem, 1)
                dve.wait_ge(rsin.sem, rsin.next(h))
                dve.wait_ge(rcos.sem, rcos.at(h, n + 1))
                dve.tensor_tensor(src[:, CTX:T], src[:, CTX:T], v.rot, ALU.add).then_inc(radd.sem, 1)
                dve.wait_ge(radd.sem, radd.next(h))

            def prep(n):
                r, t = units[n]
                w = len(blocks(t)) * P
                b = 2 * (n % 2)
                dve.wait_ge(sc.sem, sc.at(h, n + 1))
                dve.wait_ge(tp.sem, tp.at(h, n - 1))
                s = v.s[:, n % 2]
                dve.tensor_scalar(s[:, 0:CTX], ps[:, b, 0:CTX], SC, None, ALU.mult).then_inc(sm.sem, 1)
                dve.wait_ge(sm.sem, sm.next(h))
                if window(t):
                    lo, hi = window(t)
                    o = (lo - (t - 1)) * P
                    ww = (hi + 1 - lo) * P
                    dve.scalar_tensor_tensor(s[:, CTX:CTX + ww], ps[:, b + 1, 0:ww], SC, env.band[:, o:o + ww],
                                             ALU.mult, ALU.add).then_inc(sm.sem, 1)
                    dve.wait_ge(sm.sem, sm.next(h))
                dve.wait_ge(ex.sem, ex.at(h, 2 * n - 2))
                dve.tensor_reduce(v.mx[:, n % 2, 3:4], s[:, 0:w], AX.X, ALU.max).then_inc(sm.sem, 1)
                dve.wait_ge(sm.sem, sm.next(h))
                dve.tensor_scalar(v.mx[:, n % 2, 0:1], v.mx[:, n % 2, 3:4], v.skh[:, r:r + 1], -1.0,
                                  ALU.max, ALU.mult).then_inc(sm.sem, 1)
                dve.wait_ge(sm.sem, sm.next(h))

            def normalise(n):
                w = len(blocks(units[n][1])) * P
                dve.wait_ge(ex.sem, ex.at(h, 2 * n + 2))
                m = v.mx[:, n % 2]
                dve.tensor_tensor(m[:, 1:2], m[:, 1:2], m[:, 2:3], ALU.add).then_inc(pn.sem, 1)
                dve.wait_ge(pn.sem, pn.next(h))
                dve.reciprocal(m[:, 1:2], m[:, 1:2]).then_inc(pn.sem, 1)
                dve.wait_ge(pn.sem, pn.next(h))
                dve.tensor_scalar(v.s[:, n % 2, 0:w], v.s[:, n % 2, 0:w], m[:, 1:2], None, ALU.mult).then_inc(pn.sem, 1)
                dve.wait_ge(pn.sem, pn.next(h))

            def gate(n):
                r, t = units[n]
                pb = (r % 2) * AHD
                dve.wait_ge(pv.sem, pv.at(h, n + 1))
                if n == 0:
                    dve.wait_ge(st.sem, st.at(h, 0))
                    dve.wait_ge(zev.sem, zev.at(h))
                c = slice(t * P, (t + 1) * P)
                dve.tensor_tensor(v.gt[pb:pb + AHD, r // 2, c], ps[pb:pb + AHD, 6 + n % 2, 0:P],
                                  v.sz[pb:pb + AHD, r // 2, c], ALU.mult).then_inc(og.sem, 1)
                dve.wait_ge(og.sem, og.next(h))

            for n in range(NU + 3):
                if n < NU:
                    prep(n)
                if 1 <= n <= NU:
                    normalise(n - 1)
                if n >= 3:
                    gate(n - 3)

    def gpsimd(pool):
        pool.wait_ge(skl.sem, skl.at(0))
        with pool.Fori(0, AKV) as h:
            pool.wait_ge(ex.sem, ex.at(h, 0))
            pool.wait_ge(sm.sem, sm.at(h, 0))
            hold(env, pool)
            pool.tensor_copy(v.skh, v.sk[:, ds(4 * h, 4)]).then_inc(stage.sem, 1)
            pool.wait_ge(stage.sem, stage.next(h))
            for n, (src, need) in enumerate(((v.q[:, 0], 2), (v.q[:, 1], 4), (v.k, 6))):
                pool.wait_ge(qev.sem, qev.at(h, need))
                pool.wait_ge(perm.sem, perm.at(h, n + 1))
                pool.tensor_tensor(src[:, CTX:T], src[:, CTX:T], env.cos, ALU.mult).then_inc(rcos.sem, 1)
                pool.wait_ge(rcos.sem, rcos.next(h))

    sm.per = sm_at(NU - 1, 4)
    sm.base += 0
    return dict(sync=sync, tensor=tensor, scalar=scalar, vector=vector, gpsimd=gpsimd)


def out_phase(env, l):
    a = env.a
    name = ("gdn", "lru", "att", "gdn")[l]
    KC = 16 if name == "gdn" else 8
    w_out = a[name + "_w_out"][l // 3].rearrange("(k p) n -> p k n", p=P)
    last = l == DEPTH - 1
    tiles = list(range(CT, NT)) + ([] if last else list(range(CT)))
    v = carve(env, [("g", (KC, T)), ("w", (KC, D))])
    wf = env.W[:].rearrange("p a b c -> p (a b c)")
    gb = wf[:, 0:2 * D].rearrange("p (s n) -> p s n", s=2)
    dg = wf[:, 2 * D:2 * D + 2 * 512].rearrange("p (i n) -> p i n", i=2)
    yt = wf[:, 4 * D:6 * D].rearrange("p (i n) -> p i n", i=2)
    NGRP = KC // 4
    ld = [Sig(env, f"out_ld{i}", 8, 16) for i in range(NGRP)]
    dgd = Sig(env, "out_dgd", 16)
    gbm = Sig(env, "out_gbm", 4)
    gbe = Sig(env, "out_gbe", 4)
    mmd = Sig(env, "out_mm", len(tiles))
    sqd = Sig(env, f"out_sq{len(tiles)}", 3 * len(tiles))
    std = Sig(env, f"out_st{len(tiles)}", 5 * len(tiles))
    xad = Sig(env, f"out_xa{len(tiles)}", len(tiles))

    def sync(sp):
        for k in range(KC):
            sp.dma_start(v.g[:, k], a["scratch"][k]).then_inc(ld[k // 4].sem, 16)
            sp.dma_start(v.w[:, k], w_out[:, k]).then_inc(ld[k // 4].sem, 16)

    def bank(t):
        return 2 * ((t - CT) if t >= CT else t)

    def tensor(pe):
        ps = env.ps
        for n in range(4):
            pe.wait_ge(dgd.sem, dgd.at(0, 4 * n + 4))
            pe.matmul(ps[:, n, :], env.ones, dg[:, n % 2], start=True, stop=True).then_inc(gbm.sem, 1)
        pe.wait_ge(gbe.sem, gbe.at(0))
        for k in range(KC):
            if k % 4 == 0:
                pe.wait_ge(ld[k // 4].sem, ld[k // 4].at(0))
            for t in range(CT, NT):
                for i in range(2):
                    mm = pe.matmul(ps[:, bank(t) + i, :], v.g[:, k, t * P:(t + 1) * P], v.w[:, k, i * 512:(i + 1) * 512],
                                   start=(k == 0), stop=(k == KC - 1))
                if k == KC - 1:
                    mm.then_inc(mmd.sem, 1)
        if not last:
            for t in range(CT):
                pe.wait_ge(std.sem, std.at(0, 5 * (t + 1)))
                for i in range(2):
                    for k in range(KC):
                        mm = pe.matmul(ps[:, bank(t) + i, :], v.g[:, k, t * P:(t + 1) * P], v.w[:, k, i * 512:(i + 1) * 512],
                                       start=(k == 0), stop=(k == KC - 1))
                mm.then_inc(mmd.sem, 1)

    def scalar(act):
        for n in range(4):
            act.wait_ge(gbm.sem, gbm.at(0, n + 1))
            act.copy(gb[:, n // 2, (n % 2) * 512:(n % 2 + 1) * 512], env.ps[:, n, :]).then_inc(gbe.sem, 1)
            act.wait_ge(gbe.sem, gbe.next(0))
        for n, t in enumerate(tiles):
            act.wait_ge(mmd.sem, mmd.at(0, n + 1))
            act.wait_ge(xad.sem, xad.at(0, n - 1))
            for i in range(2):
                act.activation(yt[:, n % 2, i * 512:(i + 1) * 512], env.ps[:, bank(t) + i, :], ACT.Square,
                               accum_out=env.stat[:, 4, 2 * n + i:2 * n + i + 1]).then_inc(sqd.sem, 1)
                act.wait_ge(sqd.sem, sqd.next(0))
            act.wait_ge(std.sem, std.at(0, 5 * n + 2))
            act.activation(env.stat[:, 6, n:n + 1], env.stat[:, 5, n:n + 1], ACT.Sqrt).then_inc(sqd.sem, 1)
            act.wait_ge(sqd.sem, sqd.next(0))

    def vector(dve):
        for n in range(4):
            s = n // 2
            dve.wait_ge(gbm.sem, gbm.at(0, n - 1))
            for i in range(4):
                k = (n % 2) * 4 + i
                dve.tensor_scalar(dg[:, n % 2, i * P:(i + 1) * P], env.ident, env.gmul[:, l, k, s:s + 1], None,
                                  ALU.mult).then_inc(dgd.sem, 1)
                dve.wait_ge(dgd.sem, dgd.next(0))
        dve.wait_ge(gbe.sem, gbe.at(0))
        for n, t in enumerate(tiles):
            st = lambda r: env.stat[:, r, n:n + 1]
            dve.wait_ge(sqd.sem, sqd.at(0, 3 * n + 2))
            dve.tensor_tensor(st(5), env.stat[:, 4, 2 * n:2 * n + 1], env.stat[:, 4, 2 * n + 1:2 * n + 2], ALU.add).then_inc(std.sem, 1)
            dve.wait_ge(std.sem, std.next(0))
            dve.tensor_scalar(st(5), st(5), 1.0 / D, EPS, ALU.mult, ALU.add).then_inc(std.sem, 1)
            dve.wait_ge(std.sem, std.next(0))
            dve.wait_ge(sqd.sem, sqd.at(0, 3 * n + 3))
            dve.reciprocal(st(7), st(6)).then_inc(std.sem, 1)
            dve.wait_ge(std.sem, std.next(0))
            for i in range(2):
                c = slice(i * 512, (i + 1) * 512)
                dve.scalar_tensor_tensor(yt[:, n % 2, c], env.ps[:, bank(t) + i, :], st(7),
                                         gb[:, 0 if t >= CT else 1, c], ALU.mult, ALU.mult).then_inc(std.sem, 1)
                dve.wait_ge(std.sem, std.next(0))

    def gpsimd(pool):
        for n, t in enumerate(tiles):
            pool.wait_ge(std.sem, std.at(0, 5 * n + 5))
            pool.tensor_tensor(env.x[:, t], env.x[:, t], yt[:, n % 2], ALU.add).then_inc(xad.sem, 1)
            pool.wait_ge(xad.sem, xad.next(0))

    return dict(sync=sync, tensor=tensor, scalar=scalar, vector=vector, gpsimd=gpsimd)


def store_phase(env):
    out_s = Sig(env, "stored", 1, 16)

    def sync(sp):
        sp.dma_start(env.a["out"].rearrange("o (t p) d -> p (o t) d", p=P), env.x[:, CT:NT, :]).then_inc(out_s.sem, 16)
        sp.wait_ge(out_s.sem, out_s.at(0))

    return dict(sync=sync)


_INS = ["x", "c", "ctx", "c_ctx", "ada_w", "ada_b", "norm_pre", "norm_post", "gdn_w_in", "gdn_conv_w", "gdn_a_log",
        "gdn_dt_bias", "gdn_g_norm", "gdn_w_out", "lru_w_in", "lru_conv_w", "lru_conv_b", "lru_w_ra", "lru_b_ra",
        "lru_w_ri", "lru_b_ri", "lru_lam", "lru_w_out", "att_w_in", "att_sinks", "att_w_out"]


def kernel(**inputs):
    import concourse.bacc as _bacc
    from concourse.bass_utils import run_bass_kernel_spmd as _run

    nc = _bacc.Bacc("TRN2", target_bir_lowering=False, num_devices=1)
    cst, mask = shape_constants()
    arrays, aps = {}, {}
    for name in _INS:
        arrays[f"in_{name}"] = np.ascontiguousarray(inputs[name])
        aps[name] = nc.dram_tensor(f"in_{name}", arrays[f"in_{name}"].shape, F32, kind="ExternalInput").ap()
    for name, arr, dt in (("cst", cst, F32), ("mask", mask, U32)):
        arrays[f"in_{name}"] = arr
        aps[name] = nc.dram_tensor(f"in_{name}", arr.shape, dt, kind="ExternalInput").ap()
    aps["scratch"] = nc.dram_tensor("gated", (16, P, T), F32).ap()
    aps["out"] = nc.dram_tensor("out_0", (1, SEQ, D), F32, kind="ExternalOutput").ap()
    build(nc, aps)
    return _run(nc, [arrays], core_ids=[0]).results[0]["out_0"]
```
